# Optimizing a Trainium2 kernel written in Bass

```python
import jax
import jax.numpy as jnp
from jax import lax
import numpy as np
import math
import jax, jax.numpy as jnp

D_MODEL = 1024
BATCH = 1
SEQ = 512
DEPTH = 2

MLSTM_HEADS = 4
MLSTM_DH = 64
MLSTM_CHUNK = 64
CONV_K = 4
HGRN_HEADS = 4
HGRN_DK = 64
HGRN_DV = 64
HGRN_CHUNK = 32
SWA_Q_HEADS = 8
SWA_KV_HEADS = 2
SWA_DH = 64
WINDOW = 128
ROPE_THETA = 500000.0
ROT_DIM = SWA_DH // 4
D_FF = 4 * D_MODEL
PLE_DIM = 256
EPS = 1e-6

MLSTM_W = MLSTM_HEADS * MLSTM_DH
HGRN_KW = HGRN_HEADS * HGRN_DK
HGRN_VW = HGRN_HEADS * HGRN_DV
SWA_QW = SWA_Q_HEADS * SWA_DH
SWA_KVW = SWA_KV_HEADS * SWA_DH
MIX_W = MLSTM_W + HGRN_VW + SWA_QW
IN_SPLITS = (MLSTM_W, MLSTM_W, MLSTM_W, MLSTM_W, MLSTM_HEADS, MLSTM_HEADS,
             HGRN_KW, HGRN_KW, HGRN_VW, HGRN_VW, SWA_QW, SWA_KVW, SWA_KVW)
IN_W = 4 * MLSTM_W + 2 * MLSTM_HEADS + 2 * HGRN_KW + 2 * HGRN_VW + SWA_QW + 2 * SWA_KVW


def _rms_norm(x, g):
    xf = x.astype(jnp.float32)
    y = xf * lax.rsqrt(jnp.mean(xf * xf, axis=-1, keepdims=True) + EPS) * g.astype(jnp.float32)
    return y.astype(x.dtype)

def _head_rms_norm(x, g, n_heads):
    B, S, W = x.shape
    d = W // n_heads
    y = _rms_norm(x.reshape(B, S, n_heads, d), g.reshape(n_heads, d))
    return y.reshape(B, S, W)

def _split_cols(y, sizes):
    out = []
    o = 0
    for s in sizes:
        out.append(y[..., o:o + s])
        o += s
    return out

def _heads(t, n_heads):
    B, S, W = t.shape
    return t.reshape(B, S, n_heads, W // n_heads)

def _to_chunks(t, L):
    B, S, H = t.shape[:3]
    t = t.reshape((B, S // L, L, H) + t.shape[3:])
    return jnp.moveaxis(t, (1, 3), (0, 2))

def _from_chunks(t):
    nc, B, H, L, d = t.shape
    return jnp.moveaxis(t, (0, 2), (1, 3)).reshape(B, nc * L, H * d)

def _causal_conv(u, w, b):
    K = w.shape[0]
    y = lax.conv_general_dilated(u, w[:, None, :].astype(u.dtype), window_strides=(1,),
                                 padding=[(K - 1, 0)], dimension_numbers=('NWC', 'WIO', 'NWC'),
                                 feature_group_count=u.shape[-1])
    return y + b.astype(u.dtype)

def _rope_tables(positions):
    inv_freq = ROPE_THETA ** (-jnp.arange(0, ROT_DIM, 2, dtype=jnp.float32) / ROT_DIM)
    ang = positions.astype(jnp.float32)[..., None] * inv_freq
    return jnp.cos(ang)[:, :, None, :], jnp.sin(ang)[:, :, None, :]

def _partial_rope(x, cos, sin):
    xf = x.astype(jnp.float32)
    half = ROT_DIM // 2
    x1, x2, rest = xf[..., :half], xf[..., half:ROT_DIM], xf[..., ROT_DIM:]
    y = jnp.concatenate([x1 * cos - x2 * sin, x2 * cos + x1 * sin, rest], axis=-1)
    return y.astype(x.dtype)

def mlstm_chunkwise(q, k, v, i_pre, f_pre):
    f32 = jnp.float32
    B, S, H, dk = q.shape
    dv = v.shape[-1]
    L = MLSTM_CHUNK
    xs = (_to_chunks(q.astype(f32), L), _to_chunks(k.astype(f32), L), _to_chunks(v.astype(f32), L),
          _to_chunks(i_pre.astype(f32), L), _to_chunks(jax.nn.log_sigmoid(f_pre.astype(f32)), L))
    causal = jnp.tril(jnp.ones((L, L), dtype=bool))

    def step(carry, inp):
        C, n, m = carry
        q_, k_, v_, i_, lf = inp
        b = jnp.cumsum(lf, axis=-1)
        dmat = jnp.where(causal, b[..., :, None] - b[..., None, :] + i_[..., None, :], -jnp.inf)
        inter = b + m[..., None]
        m_j = jnp.maximum(inter, jnp.max(dmat, axis=-1))
        w_intra = jnp.exp(dmat - m_j[..., None])
        w_inter = jnp.exp(inter - m_j)
        s = jnp.einsum('bhld,bhsd->bhls', q_, k_) * w_intra
        num = jnp.einsum('bhls,bhse->bhle', s, v_) + w_inter[..., None] * jnp.einsum('bhld,bhde->bhle', q_, C)
        den = jnp.sum(s, axis=-1) + w_inter * jnp.einsum('bhld,bhd->bhl', q_, n)
        h = num / jnp.maximum(jnp.abs(den), jnp.exp(-m_j))[..., None]
        m_new = m_j[..., -1]
        w_s = jnp.exp(b[..., -1:] - b + i_ - m_new[..., None])
        decay = jnp.exp(b[..., -1] + m - m_new)
        C_new = decay[..., None, None] * C + jnp.einsum('bhs,bhsd,bhse->bhde', w_s, k_, v_)
        n_new = decay[..., None] * n + jnp.einsum('bhs,bhsd->bhd', w_s, k_)
        return (C_new, n_new, m_new), h

    init = (jnp.zeros((B, H, dk, dv), f32), jnp.zeros((B, H, dk), f32), jnp.zeros((B, H), f32))
    _, h = lax.scan(step, init, xs)
    return _from_chunks(h)

def hgrn2_chunkwise(q, f_pre, inp, lb):
    f32 = jnp.float32
    B, S, H, dk = q.shape
    dv = inp.shape[-1]
    L = HGRN_CHUNK
    fp = f_pre.astype(f32)
    lb = lb.astype(f32)
    log_f = jnp.logaddexp(jnp.log(lb), jnp.log1p(-lb) + jax.nn.log_sigmoid(fp))
    key = (1.0 - lb) * jax.nn.sigmoid(-fp)
    qf = jax.nn.silu(q.astype(f32))
    xs = (_to_chunks(qf, L), _to_chunks(key, L), _to_chunks(inp.astype(f32), L), _to_chunks(log_f, L))
    causal = jnp.tril(jnp.ones((L, L), dtype=bool))[:, :, None]

    def step(S_state, chunk):
        q_, k_, v_, lf = chunk
        G = jnp.cumsum(lf, axis=2)
        inter = jnp.einsum('bhld,bhde->bhle', q_ * jnp.exp(G), S_state)
        diff = G[:, :, :, None, :] - G[:, :, None, :, :]
        decay = jnp.exp(jnp.where(causal, diff, -jnp.inf))
        A = jnp.einsum('bhld,bhlsd,bhsd->bhls', q_, decay, k_)
        o = inter + jnp.einsum('bhls,bhse->bhle', A, v_)
        G_last = G[:, :, -1]
        S_new = jnp.exp(G_last)[..., None] * S_state + jnp.einsum(
            'bhsd,bhse->bhde', k_ * jnp.exp(G_last[:, :, None] - G), v_)
        return S_new, o

    _, o = lax.scan(step, jnp.zeros((B, H, dk, dv), f32), xs)
    return _from_chunks(o)

def swa_sink_attention(q, k, v, sinks):
    B, S, HQ, d = q.shape
    HKV = k.shape[2]
    G = HQ // HKV
    W = WINDOW
    nb = S // W
    qb = q.reshape(B, nb, W, HKV, G, d)
    kb = k.reshape(B, nb, W, HKV, d)
    vb = v.reshape(B, nb, W, HKV, d)
    kk = jnp.concatenate([jnp.concatenate([jnp.zeros_like(kb[:, :1]), kb[:, :-1]], axis=1), kb], axis=2)
    vv = jnp.concatenate([jnp.concatenate([jnp.zeros_like(vb[:, :1]), vb[:, :-1]], axis=1), vb], axis=2)
    s = jnp.einsum('bnqhgd,bnkhd->bnhgqk', qb, kk).astype(jnp.float32) * (d ** -0.5)
    qi = jnp.arange(W)[:, None]
    ki = jnp.arange(2 * W)[None, :]
    blk = jnp.arange(nb)[:, None, None]
    mask = (ki > qi) & (ki <= qi + W) & ((blk > 0) | (ki >= W))
    s = jnp.where(mask[None, :, None, None], s, -jnp.inf)
    sink = sinks.astype(jnp.float32).reshape(HKV, G)[None, None, :, :, None, None]
    m = jnp.maximum(jnp.max(s, axis=-1, keepdims=True), sink)
    pexp = jnp.exp(s - m)
    probs = pexp / (jnp.sum(pexp, axis=-1, keepdims=True) + jnp.exp(sink - m))
    o = jnp.einsum('bnhgqk,bnkhd->bnqhgd', probs.astype(v.dtype), vv)
    return o.reshape(B, S, HQ * d)

def first_inputs(seed: int = 0) -> dict:
    key = jax.random.key(seed)
    ks = jax.random.split(key, 24)
    f32 = jnp.float32
    nrm = lambda k, shape, scale: jax.random.normal(k, shape, f32) * scale
    x = nrm(ks[0], (BATCH, SEQ, D_MODEL), 1.0)
    p = nrm(ks[1], (DEPTH, BATCH, SEQ, PLE_DIM), 1.0)
    start = jax.random.randint(ks[2], (BATCH, 1), 0, 4096, dtype=jnp.int32)
    positions = (start + jnp.arange(SEQ, dtype=jnp.int32)[None, :]).astype(jnp.int32)
    return {
        "x": x,
        "p": p,
        "positions": positions,
        "in_norm_g": 1.0 + nrm(ks[3], (DEPTH, D_MODEL), 0.05),
        "w_in": nrm(ks[4], (DEPTH, D_MODEL, IN_W), D_MODEL ** -0.5),
        "b_in": nrm(ks[5], (DEPTH, IN_W), 0.02),
        "mlstm_f_bias": jnp.linspace(3.0, 6.0, MLSTM_HEADS, dtype=f32)[None, :] + nrm(ks[6], (DEPTH, MLSTM_HEADS), 0.1),
        "mlstm_conv_w": nrm(ks[7], (DEPTH, CONV_K, 2 * MLSTM_W), CONV_K ** -0.5),
        "mlstm_conv_b": nrm(ks[8], (DEPTH, 2 * MLSTM_W), 0.02),
        "mlstm_norm_g": 1.0 + nrm(ks[9], (DEPTH, MLSTM_W), 0.05),
        "hgrn_lb_logits": nrm(ks[10], (DEPTH, HGRN_KW), 0.1),
        "hgrn_norm_g": 1.0 + nrm(ks[11], (DEPTH, HGRN_VW), 0.05),
        "swa_q_norm_g": 1.0 + nrm(ks[12], (DEPTH, SWA_DH), 0.05),
        "swa_k_norm_g": 1.0 + nrm(ks[13], (DEPTH, SWA_DH), 0.05),
        "swa_sinks": nrm(ks[14], (DEPTH, SWA_Q_HEADS), 0.5),
        "w_out": nrm(ks[15], (DEPTH, MIX_W, D_MODEL), MIX_W ** -0.5),
        "mlp_norm_g": 1.0 + nrm(ks[16], (DEPTH, D_MODEL), 0.05),
        "w_up": nrm(ks[17], (DEPTH, D_MODEL, D_FF), D_MODEL ** -0.5),
        "w_down": nrm(ks[18], (DEPTH, D_FF, D_MODEL), D_FF ** -0.5),
        "ple_norm_g": 1.0 + nrm(ks[19], (DEPTH, D_MODEL), 0.05),
        "w_ple_gate": nrm(ks[20], (DEPTH, D_MODEL, D_MODEL), D_MODEL ** -0.5),
        "w_ple_proj": nrm(ks[21], (DEPTH, PLE_DIM, D_MODEL), PLE_DIM ** -0.5),
        "ple_post_norm_g": 1.0 + nrm(ks[22], (DEPTH, D_MODEL), 0.05),
    }

def first_block(x, p, positions, in_norm_g, w_in, b_in, mlstm_f_bias, mlstm_conv_w, mlstm_conv_b,
              mlstm_norm_g, hgrn_lb_logits, hgrn_norm_g, swa_q_norm_g, swa_k_norm_g, swa_sinks,
              w_out, mlp_norm_g, w_up, w_down, ple_norm_g, w_ple_gate, w_ple_proj, ple_post_norm_g):
    cos, sin = _rope_tables(positions)
    lb_all = jnp.cumsum(jax.nn.softmax(hgrn_lb_logits.astype(jnp.float32), axis=0), axis=0)
    lb_all = lb_all - lb_all[0:1]
    B, S, _ = x.shape
    for l in range(DEPTH):
        h = _rms_norm(x, in_norm_g[l])
        y = h @ w_in[l] + b_in[l]
        (mq, mk, mv, mo, mi, mf, hq, hf, hi, hg, sq, sk, sv) = _split_cols(y, IN_SPLITS)

        qk = jax.nn.silu(_causal_conv(jnp.concatenate([mq, mk], axis=-1), mlstm_conv_w[l], mlstm_conv_b[l]))
        mq_c, mk_c = qk[..., :MLSTM_W], qk[..., MLSTM_W:]
        m_h = mlstm_chunkwise(_heads(mq_c, MLSTM_HEADS), _heads(mk_c, MLSTM_HEADS) * (MLSTM_DH ** -0.5),
                              _heads(mv, MLSTM_HEADS), mi, mf + mlstm_f_bias[l])
        m_out = (_head_rms_norm(m_h, mlstm_norm_g[l], MLSTM_HEADS)
                 * jax.nn.sigmoid(mo.astype(jnp.float32))).astype(x.dtype)

        h_h = hgrn2_chunkwise(_heads(hq, HGRN_HEADS), _heads(hf, HGRN_HEADS), _heads(hi, HGRN_HEADS),
                              lb_all[l].reshape(HGRN_HEADS, HGRN_DK))
        h_out = (_head_rms_norm(h_h, hgrn_norm_g[l], HGRN_HEADS)
                 * jax.nn.silu(hg.astype(jnp.float32))).astype(x.dtype)

        q_s = _partial_rope(_rms_norm(_heads(sq, SWA_Q_HEADS), swa_q_norm_g[l]), cos, sin)
        k_s = _partial_rope(_rms_norm(_heads(sk, SWA_KV_HEADS), swa_k_norm_g[l]), cos, sin)
        s_out = swa_sink_attention(q_s, k_s, _heads(sv, SWA_KV_HEADS), swa_sinks[l]).astype(x.dtype)

        x = x + jnp.concatenate([m_out, h_out, s_out], axis=-1) @ w_out[l]

        u = _rms_norm(x, mlp_norm_g[l]) @ w_up[l]
        x = x + jnp.square(jax.nn.relu(u)) @ w_down[l]

        gate = jax.nn.sigmoid((_rms_norm(x, ple_norm_g[l]) @ w_ple_gate[l]).astype(jnp.float32))
        e = _rms_norm(p[l] @ w_ple_proj[l], ple_post_norm_g[l]).astype(jnp.float32)
        x = x + (gate * e).astype(x.dtype)
    return x


N_MEM = 256
HEAD_DIM = 64
ROT_DIM_2 = HEAD_DIM // 4
NEG_INF = -1e30
N_MIXERS = 3

A_HEADS = D_MODEL // HEAD_DIM
A_WIDTH = A_HEADS * HEAD_DIM
A_PATTERNS = ((128, 1), (512, 4), (2048, 16))
A_BLOCK = 64

B_HEADS = D_MODEL // (2 * HEAD_DIM)
B_WIDTH = B_HEADS * 2 * HEAD_DIM
B_QBLOCK = 128

C_HEADS = D_MODEL // HEAD_DIM
C_KV_HEADS = max(1, C_HEADS // 8)
C_GROUP = C_HEADS // C_KV_HEADS
C_Q_WIDTH = C_HEADS * HEAD_DIM
C_KV_WIDTH = C_KV_HEADS * HEAD_DIM
C_RADIUS = 128
C_BLOCK = 128

X_HEADS = 4
X_HEAD_DIM = D_MODEL // X_HEADS

_FF_RAW = -(-8 * D_MODEL // 3)
D_FF_2 = -(-_FF_RAW // 256) * 256

N_A = len(range(0, DEPTH, N_MIXERS))
N_B = len(range(1, DEPTH, N_MIXERS))
N_C = len(range(2, DEPTH, N_MIXERS))


def rms_norm(x, g):
    xf = x.astype(jnp.float32)
    y = xf * lax.rsqrt(jnp.mean(xf * xf, axis=-1, keepdims=True) + EPS)
    return (y * g.astype(jnp.float32)).astype(x.dtype)

def split_heads(t, n):
    b, s, _ = t.shape
    return t.reshape(b, s, n, -1).transpose(0, 2, 1, 3)

def merge_heads(t):
    b, n, s, d = t.shape
    return t.transpose(0, 2, 1, 3).reshape(b, s, n * d)

def rope_tables(positions):
    inv_freq = ROPE_THETA ** (-jnp.arange(0, ROT_DIM_2, 2, dtype=jnp.float32) / ROT_DIM_2)
    ang = positions.astype(jnp.float32)[..., None] * inv_freq
    return jnp.cos(ang), jnp.sin(ang)

def apply_partial_rope(t, cos, sin):
    shape = (cos.shape[0],) + (1,) * (t.ndim - 3) + cos.shape[1:]
    c = cos.reshape(shape).astype(t.dtype)
    s = sin.reshape(shape).astype(t.dtype)
    half = ROT_DIM_2 // 2
    t1, t2, rest = t[..., :half], t[..., half:ROT_DIM_2], t[..., ROT_DIM_2:]
    return jnp.concatenate([t1 * c - t2 * s, t2 * c + t1 * s, rest], axis=-1)

def banded_attention(q, k, v, radius, block, sink=None):
    L = q.shape[-2]
    nb = -(-L // block)
    pad = nb * block - L

    def pad_seq(t, lo, hi):
        return jnp.pad(t, [(0, 0)] * (t.ndim - 2) + [(lo, hi), (0, 0)])

    qb = pad_seq(q, 0, pad).reshape(q.shape[:-2] + (nb, block, q.shape[-1]))

    def band(t):
        tp = pad_seq(t, block, block + pad).reshape(t.shape[:-2] + (nb + 2, block, t.shape[-1]))
        return jnp.concatenate([tp[..., :-2, :, :], tp[..., 1:-1, :, :], tp[..., 2:, :, :]], axis=-2)

    kb, vb = band(k), band(v)
    s = jnp.einsum('...gnqd,...nkd->...gnqk', qb, kb,
                   preferred_element_type=jnp.float32) * (q.shape[-1] ** -0.5)
    qpos = jnp.arange(nb * block).reshape(nb, block, 1)
    kpos = (jnp.arange(nb)[:, None, None] - 1) * block + jnp.arange(3 * block)[None, None, :]
    valid = (jnp.abs(kpos - qpos) <= radius) & (kpos >= 0) & (kpos < L)
    s = jnp.where(valid, s, NEG_INF)
    m = jnp.max(s, axis=-1, keepdims=True)
    if sink is not None:
        sink = sink.astype(jnp.float32)
        m = jnp.maximum(m, sink)
    p = jnp.exp(s - m)
    denom = jnp.sum(p, axis=-1, keepdims=True)
    if sink is not None:
        denom = denom + jnp.exp(sink - m)
    o = jnp.einsum('...gnqk,...nkd->...gnqd', p.astype(v.dtype), vb,
                   preferred_element_type=jnp.float32) / denom
    lse = (m + jnp.log(denom))[..., 0]
    o = o.reshape(o.shape[:-3] + (nb * block, o.shape[-1]))[..., :L, :]
    lse = lse.reshape(lse.shape[:-2] + (nb * block,))[..., :L]
    return o, lse

def dilated_attention_mixer(u, w_in, w_out, cos, sin):
    b, s_len, _ = u.shape
    q, k, v = jnp.split(u @ w_in, 3, axis=-1)
    q = apply_partial_rope(split_heads(q, A_HEADS), cos, sin)
    k = apply_partial_rope(split_heads(k, A_HEADS), cos, sin)
    v = split_heads(v, A_HEADS)
    outs, lses = [], []
    for window, dil in A_PATTERNS:
        radius = window // (2 * dil)

        def by_residue(t):
            return t.reshape(b, A_HEADS, s_len // dil, dil, HEAD_DIM).swapaxes(2, 3)

        o, lse = banded_attention(by_residue(q)[..., None, :, :], by_residue(k), by_residue(v),
                                  radius, A_BLOCK)
        outs.append(o[..., 0, :, :].swapaxes(2, 3).reshape(b, A_HEADS, s_len, HEAD_DIM))
        lses.append(lse[..., 0, :].swapaxes(2, 3).reshape(b, A_HEADS, s_len))
    w = jax.nn.softmax(jnp.stack(lses), axis=0)
    o = jnp.einsum('pbhs,pbhsd->bhsd', w, jnp.stack(outs))
    return merge_heads(o).astype(u.dtype) @ w_out

def differential_attention_mixer(u, w_in, w_out, lam_q1, lam_k1, lam_q2, lam_k2, sub_g,
                                 cos, sin, layer_idx):
    b, s_len, _ = u.shape
    q, k, v = jnp.split(u @ w_in, 3, axis=-1)

    def qk_heads(t):
        return t.reshape(b, s_len, B_HEADS, 2, HEAD_DIM).transpose(0, 2, 3, 1, 4)

    q = apply_partial_rope(qk_heads(q), cos, sin)
    k = apply_partial_rope(qk_heads(k), cos, sin)
    v = split_heads(v, B_HEADS)
    lam_init = 0.8 - 0.6 * math.exp(-0.3 * layer_idx)
    f32 = jnp.float32
    lam = (jnp.exp(jnp.sum(lam_q1.astype(f32) * lam_k1.astype(f32)))
           - jnp.exp(jnp.sum(lam_q2.astype(f32) * lam_k2.astype(f32))) + lam_init)
    nqb = s_len // B_QBLOCK
    qb = q.reshape(b, B_HEADS, 2, nqb, B_QBLOCK, HEAD_DIM).transpose(3, 0, 1, 2, 4, 5)
    scale = HEAD_DIM ** -0.5

    def one_block(qblk):
        sc = jnp.einsum('bhcqd,bhckd->bhcqk', qblk, k, preferred_element_type=f32) * scale
        p = jax.nn.softmax(sc, axis=-1)
        a = p[:, :, 0] - lam * p[:, :, 1]
        return jnp.einsum('bhqk,bhkd->bhqd', a.astype(v.dtype), v, preferred_element_type=f32)

    o = lax.map(one_block, qb)
    o = o.transpose(1, 2, 0, 3, 4).reshape(b, B_HEADS, s_len, 2 * HEAD_DIM)
    o = rms_norm(o, sub_g) * (1.0 - lam_init)
    return merge_heads(o).astype(u.dtype) @ w_out

def windowed_gqa_sink_mixer(u, w_in, w_out, sink, cos, sin):
    b, s_len, _ = u.shape
    qkv = u @ w_in
    q = qkv[..., :C_Q_WIDTH]
    k = qkv[..., C_Q_WIDTH:C_Q_WIDTH + C_KV_WIDTH]
    v = qkv[..., C_Q_WIDTH + C_KV_WIDTH:]
    q = apply_partial_rope(split_heads(q, C_HEADS), cos, sin)
    k = apply_partial_rope(split_heads(k, C_KV_HEADS), cos, sin)
    v = split_heads(v, C_KV_HEADS)
    q = q.reshape(b, C_KV_HEADS, C_GROUP, s_len, HEAD_DIM)
    o, _ = banded_attention(q, k, v, C_RADIUS, C_BLOCK,
                            sink=sink.reshape(1, C_KV_HEADS, C_GROUP, 1, 1, 1))
    o = o.reshape(b, C_HEADS, s_len, HEAD_DIM)
    return merge_heads(o).astype(u.dtype) @ w_out

def memory_cross_attention(u, mem_n, wq, wkv, wo):
    q = split_heads(u @ wq, X_HEADS)
    k, v = jnp.split(mem_n @ wkv, 2, axis=-1)
    k = split_heads(k, X_HEADS)
    v = split_heads(v, X_HEADS)
    s = jnp.einsum('bhqd,bhkd->bhqk', q, k,
                   preferred_element_type=jnp.float32) * (X_HEAD_DIM ** -0.5)
    p = jax.nn.softmax(s, axis=-1)
    o = jnp.einsum('bhqk,bhkd->bhqd', p.astype(v.dtype), v)
    return merge_heads(o) @ wo

def swiglu_ffn(u, w_gate_up, w_down):
    g, up = jnp.split(u @ w_gate_up, 2, axis=-1)
    return (jax.nn.silu(g) * up) @ w_down

def second_inputs(seed: int = 0) -> dict:
    key = jax.random.key(seed)
    ks = iter(jax.random.split(key, 32))

    def nrm(shape, scale):
        return jax.random.normal(next(ks), shape, jnp.float32) * scale

    def dense(shape):
        return nrm(shape, shape[-2] ** -0.5)

    def gain(shape):
        return 1.0 + nrm(shape, 0.05)

    x = nrm((BATCH, SEQ, D_MODEL), 1.0)
    mem = nrm((BATCH, N_MEM, D_MODEL), 1.0)
    offset = jax.random.randint(next(ks), (BATCH, 1), 0, 4096, dtype=jnp.int32)
    positions = jnp.arange(SEQ, dtype=jnp.int32)[None, :] + offset
    return {
        "x": x, "mem": mem, "positions": positions,
        "mix_pre_g": gain((DEPTH, D_MODEL)), "mix_post_g": gain((DEPTH, D_MODEL)),
        "mem_pre_g": gain((DEPTH, D_MODEL)), "mem_kv_g": gain((DEPTH, D_MODEL)),
        "mem_post_g": gain((DEPTH, D_MODEL)),
        "ffn_pre_g": gain((DEPTH, D_MODEL)), "ffn_post_g": gain((DEPTH, D_MODEL)),
        "a_w_in": dense((N_A, D_MODEL, 3 * A_WIDTH)), "a_w_out": dense((N_A, A_WIDTH, D_MODEL)),
        "b_w_in": dense((N_B, D_MODEL, 3 * B_WIDTH)), "b_w_out": dense((N_B, B_WIDTH, D_MODEL)),
        "b_lam_q1": nrm((N_B, HEAD_DIM), 0.1), "b_lam_k1": nrm((N_B, HEAD_DIM), 0.1),
        "b_lam_q2": nrm((N_B, HEAD_DIM), 0.1), "b_lam_k2": nrm((N_B, HEAD_DIM), 0.1),
        "b_sub_g": gain((N_B, 2 * HEAD_DIM)),
        "c_w_in": dense((N_C, D_MODEL, C_Q_WIDTH + 2 * C_KV_WIDTH)),
        "c_w_out": dense((N_C, C_Q_WIDTH, D_MODEL)),
        "c_sink": nrm((N_C, C_HEADS), 0.5),
        "x_wq": dense((DEPTH, D_MODEL, D_MODEL)), "x_wkv": dense((DEPTH, D_MODEL, 2 * D_MODEL)),
        "x_wo": dense((DEPTH, D_MODEL, D_MODEL)),
        "w_gate_up": dense((DEPTH, D_MODEL, 2 * D_FF_2)), "w_down": dense((DEPTH, D_FF_2, D_MODEL)),
    }

def second_block(x, mem, positions, mix_pre_g, mix_post_g, mem_pre_g, mem_kv_g, mem_post_g,
              ffn_pre_g, ffn_post_g, a_w_in, a_w_out, b_w_in, b_w_out, b_lam_q1, b_lam_k1,
              b_lam_q2, b_lam_k2, b_sub_g, c_w_in, c_w_out, c_sink, x_wq, x_wkv, x_wo,
              w_gate_up, w_down):
    cos, sin = rope_tables(positions)
    h = x
    for i in range(DEPTH):
        kind, j = i % N_MIXERS, i // N_MIXERS
        u = rms_norm(h, mix_pre_g[i])
        if kind == 0:
            y = dilated_attention_mixer(u, a_w_in[j], a_w_out[j], cos, sin)
        elif kind == 1:
            y = differential_attention_mixer(u, b_w_in[j], b_w_out[j], b_lam_q1[j], b_lam_k1[j],
                                             b_lam_q2[j], b_lam_k2[j], b_sub_g[j], cos, sin, i)
        else:
            y = windowed_gqa_sink_mixer(u, c_w_in[j], c_w_out[j], c_sink[j], cos, sin)
        h = h + rms_norm(y, mix_post_g[i])
        u = rms_norm(h, mem_pre_g[i])
        y = memory_cross_attention(u, rms_norm(mem, mem_kv_g[i]), x_wq[i], x_wkv[i], x_wo[i])
        h = h + rms_norm(y, mem_post_g[i])
        u = rms_norm(h, ffn_pre_g[i])
        y = swiglu_ffn(u, w_gate_up[i], w_down[i])
        h = h + rms_norm(y, ffn_post_g[i])
    return h


def setup_inputs(seed=0):
    out = dict(first_inputs(seed))
    for name, value in second_inputs(seed + 1).items():
        if name != "x":
            out[name + "_2"] = value
    return out


def reference(
    x, p, positions, in_norm_g, w_in, b_in, mlstm_f_bias, mlstm_conv_w, mlstm_conv_b,
    mlstm_norm_g, hgrn_lb_logits, hgrn_norm_g, swa_q_norm_g, swa_k_norm_g, swa_sinks, w_out,
    mlp_norm_g, w_up, w_down, ple_norm_g, w_ple_gate, w_ple_proj, ple_post_norm_g, mem_2,
    positions_2, mix_pre_g_2, mix_post_g_2, mem_pre_g_2, mem_kv_g_2, mem_post_g_2, ffn_pre_g_2,
    ffn_post_g_2, a_w_in_2, a_w_out_2, b_w_in_2, b_w_out_2, b_lam_q1_2, b_lam_k1_2, b_lam_q2_2,
    b_lam_k2_2, b_sub_g_2, c_w_in_2, c_w_out_2, c_sink_2, x_wq_2, x_wkv_2, x_wo_2, w_gate_up_2,
    w_down_2,
):
    x = first_block(
        x, p, positions, in_norm_g, w_in, b_in, mlstm_f_bias, mlstm_conv_w, mlstm_conv_b,
        mlstm_norm_g, hgrn_lb_logits, hgrn_norm_g, swa_q_norm_g, swa_k_norm_g, swa_sinks, w_out,
        mlp_norm_g, w_up, w_down, ple_norm_g, w_ple_gate, w_ple_proj, ple_post_norm_g,
    )
    return second_block(
        x, mem_2, positions_2, mix_pre_g_2, mix_post_g_2, mem_pre_g_2, mem_kv_g_2, mem_post_g_2,
        ffn_pre_g_2, ffn_post_g_2, a_w_in_2, a_w_out_2, b_w_in_2, b_w_out_2, b_lam_q1_2,
        b_lam_k1_2, b_lam_q2_2, b_lam_k2_2, b_sub_g_2, c_w_in_2, c_w_out_2, c_sink_2, x_wq_2,
        x_wkv_2, x_wo_2, w_gate_up_2, w_down_2,
    )


_drawn_inputs = setup_inputs


def setup_inputs(seed=0):
    import zlib

    import numpy as np

    out = dict(_drawn_inputs(seed))
    spreads = {}
    factors = {'mlstm_conv_b': 6.901,
     'mlstm_norm_g': 3.26,
     'hgrn_lb_logits': 8.0,
     'hgrn_norm_g': 3.203,
     'swa_q_norm_g': 8.0,
     'swa_k_norm_g': 8.0,
     'swa_sinks': 47.648,
     'ple_norm_g': 7.457,
     'ple_post_norm_g': 2.795,
     'b_lam_q1_2': 64.0,
     'b_lam_k1_2': 64.0,
     'b_lam_q2_2': 200.0,
     'b_lam_k2_2': 8.0,
     'b_sub_g_2': 15.405,
     'mix_pre_g_2': 2.777,
     'mix_post_g_2': 3.032,
     'mem_pre_g_2': 3.566,
     'mem_post_g_2': 3.25,
     'ffn_post_g_2': 3.587}
    for name, (base, spread) in spreads.items():
        noise = np.random.default_rng([zlib.crc32(name.encode()), seed]).standard_normal(out[name].shape)
        drawn = base * np.exp(spread * noise) if base else spread * noise
        out[name] = jnp.asarray(drawn.astype(out[name].dtype))
    for name, factor in factors.items():
        out[name] = (out[name] * factor).astype(out[name].dtype)
    return out
```

```python
from contextlib import ExitStack

import numpy as np

import concourse.bass as bass
from concourse import mybir

F32 = mybir.dt.float32
F32R = mybir.dt.float32r
I32 = mybir.dt.int32
U8 = mybir.dt.uint8
ALU = mybir.AluOpType
ACT = mybir.ActivationFunctionType

P = 128
S = 512
ST = S // P
D = 1024
DT = D // P
MEM = 256
FF1 = 4096
FF2 = 2816
PLE = 256
LAYERS = 2
EPS = 1e-6
BIG = 1e30
KU = 8
RAW, SPLIT = 4, 2

H4, H8 = 256, 512
_O = dict(mq=0, mk=256, mv=512, mo=768, mi=1024, mf=1028, hq=1032, hf=1288, hi=1544, hg=1800,
          sq=2056, sk=2568, sv=2696)


def win_columns():
    r = lambda a, n: list(range(a, a + n))
    cols = r(_O["mq"], 256) + r(_O["mk"], 256) + r(_O["mo"], 256) + r(_O["hq"], 256)
    cols += r(_O["hf"], 256) + r(_O["hg"], 256) + r(_O["sq"], 512)
    cols += r(_O["sk"], 64) * 2 + r(_O["sk"] + 64, 64) * 2
    cols += r(_O["mv"], 256) + r(_O["hi"], 256) + r(_O["sv"], 128)
    cols += r(_O["mi"], 4) + [-1] * 28 + r(_O["mf"], 4) + [-1] * 92
    return cols


T_MQ, T_MK, T_MO, T_HQ, T_HF, T_HG, T_SQ, T_SK, T_MV, T_HI, T_SV, T_GATE = 0, 2, 4, 6, 8, 10, 12, 16, 18, 20, 22, 23
WIN_T = 24

_VECS = [("in_g", 8, 2), ("b_in", 24, 2), ("mlp_g", 8, 2), ("ple_g", 8, 2), ("post_g", 8, 2),
         ("conv_w", 16, 2), ("conv_b", 4, 2), ("m_g", 2, 2), ("h_g", 2, 2), ("q_g", 1, 2), ("k_g", 1, 2),
         ("f_b", 1, 2), ("lb_logit", 2, 2), ("sinks", 8, 2),
         ("mix_pre", 8, 2), ("mix_post", 8, 2), ("mem_pre", 8, 2), ("mem_kv", 8, 2), ("mem_post", 8, 2),
         ("ffn_pre", 8, 2), ("ffn_post", 8, 2), ("sub_g", 1, 1), ("lam", 4, 1), ("inv_freq", 1, 1)]
VCOL, NV = {}, 0
for _n, _w, _l in _VECS:
    VCOL[_n] = (NV, _w)
    NV += _w * _l

FFN1_CHUNKS = 4
FFN2_CHUNKS = (8, 8, 6)
STREAM = []
for _l in range(LAYERS):
    STREAM += [(24 + 8 + 64, 8), (8, 2), (8, 8)]
for _l in range(LAYERS):
    STREAM += [(24 + 8 + 16 + 8 + 8 + 24 + 24 + 12, 8), (8, 6)]
UNITS = sum(n for n, _ in STREAM)
X_TILES = DT * 6 * LAYERS

_TWO_PI = 2 * np.pi
C1 = 6.28125
C2 = float(np.round((_TWO_PI - C1) * 2 ** 20) / 2 ** 20)
C3 = float(np.float32(_TWO_PI - C1 - C2))
MAGIC = 1.5 * 2.0 ** 23


def constants():
    i = np.arange(P)
    rot = np.zeros((P, P), np.float32)
    for base in (0, 64):
        for d in range(8):
            rot[base + d + 8, base + d] = -1.0
            rot[base + d, base + d + 8] = 1.0
    heads = np.zeros((12, 768), np.float32)
    heads[np.arange(768) // 64, np.arange(768)] = 1.0
    halves = np.zeros((P, 22), np.float32)
    halves[:64, 10] = halves[64:, 11] = 1.0
    unit8 = np.zeros((P, 15), np.float32)
    unit8[:, 7] = 1.0
    q, k = np.arange(P)[:, None], np.arange(2 * P)[None, :]
    band = np.where((k > q) & (k <= q + P), 0.0, -BIG).astype(np.float32)
    delta = np.arange(P)[:, None] - (np.arange(896)[None, :] - 384)
    count = (abs(delta) <= 64) * 1 + ((delta % 4 == 0) & (abs(delta) <= 256)) + ((delta % 16 == 0) & (abs(delta) <= 1024))
    dilated = np.where(count > 0, 8.0 * np.log(np.maximum(count, 1)), -BIG).astype(np.float32)
    level = np.zeros((8, P, P), np.float32)
    for j in range(7):
        w = 2 ** j
        s_, l_ = i[:, None], i[None, :]
        level[j] = (s_ // (2 * w) == l_ // (2 * w)) & (s_ // w % 2 == 0) & (l_ // w % 2 == 1)
    level[7] = np.eye(P)
    tri = (i[:, None] <= i[None, :]).astype(np.float32)
    small = np.concatenate([np.eye(P, dtype=np.float32), rot, band, tri, halves, unit8], axis=1)
    return dict(c_small=small, c_heads=heads, c_dilated=dilated,
                c_level=np.ascontiguousarray(level.transpose(1, 0, 2)).reshape(P, 8 * P))


class Counts:

    def __init__(self, eng):
        self.eng, self.n, self.reg, self.per = eng, {}, None, {}
        self.unit = self.next = self.groups = self.squares = 0
        self.per_units = 0

    def count(self, sem, more=1):
        n = self.n[sem.name] = self.n.get(sem.name, 0) + more
        per = self.per.get(sem.name, 0) if self.reg is not None else 0
        return self.reg * per + n if per else n

    def by_unit(self, value, times=1):
        return self.reg * (self.per_units * times) + value if self.reg is not None else value

    def begun(self, value):
        return value > 0 or self.reg is not None

    def since(self, sem, value):
        return self.n.get(sem.name, 0) + value

    def add(self, sem, more):
        self.n[sem.name] = self.n.get(sem.name, 0) + more

    def loop(self, times, per, units):
        return _Loop(self, times, per, units)

    def pick(self, first, stride):
        return first if self.reg is None else self.reg * stride + first


class _Loop:
    def __init__(self, c, times, per, units):
        self.c, self.times, self.units = c, times, units
        self.per = {sem.name: n for sem, n in per.items()}
        self.fori = c.eng.Fori(0, times)

    def __enter__(self):
        c = self.c
        c.reg = self.fori.__enter__()
        c.per, c.per_units = self.per, self.units

    def __exit__(self, *a):
        self.fori.__exit__(*a)
        c = self.c
        c.reg = None
        for name, per in self.per.items():
            c.n[name] = c.n.get(name, 0) + (self.times - 1) * per
        c.unit += (self.times - 1) * self.units
        c.next += (self.times - 1) * self.units


class Attention:

    def __init__(self, heads, comps, scale, key_tiles, scores, mask, sink, outputs):
        self.heads, self.comps, self.scale = heads, comps, scale
        self.key_tiles, self.scores, self.mask, self.sink, self.outputs = key_tiles, scores, mask, sink, outputs
        self.groups = [(h, q) for h in range(heads) for q in range(ST)]


def build(nc, dram, out):
    ctx = ExitStack()
    with ctx:
        sem = lambda name: ctx.enter_context(nc.semaphore(name))

        top = [(nc.sbuf_base + 63) // 64 * 64]

        def place(name, shape, dt=F32, at=None):
            size = int(np.prod(shape[1:])) * (1 if dt == U8 else 4)
            if at is None:
                at, top[0] = top[0], top[0] + (size + 63) // 64 * 64
            return nc.alloc_sbuf_tensor_at(name, shape, dt, offset=at)

        def region(size):
            at, top[0] = top[0], top[0] + size
            return at

        KB = 1024
        x = place("x", [P, DT, S])
        at_a, at_b = region(32 * KB), region(32 * KB)
        a_op = (place("a_hi", [P, DT, S], F32R, at_a), place("a_lo", [P, DT, S], F32R, at_a + 16 * KB))
        b_op = (place("b_hi", [P, DT, S], F32R, at_b), place("b_lo", [P, DT, S], F32R, at_b + 16 * KB))
        w_raw = place("w_raw", [P, RAW, KU * P])
        w_hi = place("w_hi", [P, SPLIT, KU * P], F32R)
        w_lo = place("w_lo", [P, SPLIT, KU * P], F32R)
        y = place("y", [P, 24, S])
        at_o, at_v = region(16 * KB), region(16 * KB)
        o = place("o", [P, DT, S], F32, at_o)
        v = place("v", [P, ST, D], F32, at_v)
        sq = place("sq", [P, 2, S], F32, at_o)
        sq_sum = place("sq_sum", [P, S], F32, at_o + 4 * KB)
        root = place("root", [P, S], F32, at_o + 6 * KB)
        r_post = place("r_post", [P, S], F32, at_o + 8 * KB)
        mem = place("mem", [P, DT, MEM], F32, at_v)
        ple = place("ple", [P, 2, S], F32, at_v)
        small = place("small", [P, 4 * P + P + 22 + 15])
        ident, rot, band, tri = (small[:, a:b] for a, b in ((0, 128), (128, 256), (256, 512), (512, 640)))
        halves, unit8 = small[:, 640:662], small[:, 662:677]
        heads_c = place("heads_c", [12, 768])
        level = place("level", [P, 8, P], U8)
        vec = place("vec", [P, NV])
        der = place("der", [P, 64])
        r_x = place("r_x", [P, S])
        r_mem = place("r_mem", [P, MEM])
        cos_t, sin_t = place("cos_t", [P, S]), place("sin_t", [P, S])
        assert top[0] <= nc.sbuf_usable_end, (top[0], nc.sbuf_usable_end)
        eps, half_pi, ones = der[:, 0:1], der[:, 1:2], der[:, 2:3]
        lb, one_lb = der[:, 4:8], der[:, 8:12]
        neg_sink, lam, lam_e = der[:, 12:28], der[:, 28:29], der[:, 30:32]
        stat_n, stat_d, stat_s = der[:, 32:40], der[:, 40:48], der[:, 48:56]
        eps_big = der[:, 3:4]

        def in_a(name, shape, kb, dt=F32):
            return place(name, shape, dt, at_a + int(kb * KB))

        def in_b(name, shape, kb, dt=F32):
            return place(name, shape, dt, at_b + int(kb * KB))

        pos_i = in_a("pos_i", [P, S], 0, I32)
        ang = in_a("ang", [P, 3, S], 2)
        h_lp = in_a("h_lp", [P, 2, S], 0)
        h_ls = in_a("h_ls", [P, 2, S], 4)
        h_q = in_a("h_q", [P, 2, 2, S], 8)
        h_k = in_a("h_k", [P, 2, 2, S], 16)
        h_key = in_a("h_key", [P, 2, S], 24)
        h_neg = in_a("h_neg", [P, 2, S], 28)
        h_d = in_b("h_d", [P, 4, ST, P], 0)
        h_o1 = in_b("h_o1", [P, 4, 2, P], 8)
        h_o2 = in_b("h_o2", [P, 4, 2, 2 * P], 12)
        m_row = in_b("m_row", [P, 8, S], 0)
        m_end = in_b("m_end", [P, 2, S], 16)
        m_t = in_b("m_t", [P, 2, S], 20)
        m_w = in_b("m_w", [P, 2, S], 24)
        m_s = in_b("m_s", [P, 2, S], 28)
        m_col = in_a("m_col", [P, 16], 0)
        m_den = in_a("m_den", [P, 2, S], 1)
        m_rec = in_a("m_rec", [P, 2, S], 5)
        n_sq = in_a("n_sq", [P, 8, S], 0)
        n_row = in_a("n_row", [16, 2, S], 16)
        e_sq = in_a("e_sq", [P, 2, S], 24)
        prob = in_b("prob", [P, 4, S], 0)
        prob_t = in_b("prob_t", [P, 2, ST, S], 8)
        dil = in_b("dil", [P, 896], 24)
        r_t = in_a("r_t", [P, 2, S], 20)

        bank = [ctx.enter_context(nc.psum_tensor(f"bank{i}", [P, S], F32)) for i in range(8)]
        S_BANK, T_BANK, O_BANK = (0, 1, 2, 5), (3, 4), (6, 7)
        SUM_BANK = 2

        loaded, x_loaded, stored = sem("loaded"), sem("x_loaded"), sem("stored")
        w_landed = [sem(f"w_landed{i}") for i in range(RAW)]
        w_hi_ready, w_lo_ready, unit_done, bank_free = sem("w_hi_ready"), sem("w_lo_ready"), sem("unit_done"), sem("bank_free")
        x_ready, a_hi_ready, a_ready = sem("x_ready"), sem("a_hi_ready"), sem("a_ready")
        h_hi_ready, h_ready = sem("h_hi_ready"), sem("h_ready")
        act_made, f_ready, y_zero = sem("act_made"), sem("f_ready"), sem("y_zero")
        sq_ready, sq_added, sum_ready, root_ready, recip_ready = (
            sem("sq_ready"), sem("sq_added"), sem("sum_ready"), sem("root_ready"), sem("recip_ready"))
        ple_landed, mem_first_landed, mem_landed, pos_landed, dil_landed = sem("ple_landed"), sem("mem_first_landed"), sem("mem_landed"), sem("pos_landed"), sem("dil_landed")
        met = {n: sem(f"met_{n}") for n in ("pe", "act", "dve", "pool")}
        conv_made, gates_split, gates_log, gates_made, cols_made = (
            sem("conv_made"), sem("gates_split"), sem("gates_log"), sem("gates_made"), sem("cols_made"))
        m_scored, m_gap_made, m_w_made, m_w_masked, m_s_made, m_summed, m_den_made = (
            sem("m_scored"), sem("m_gap_made"), sem("m_w_made"), sem("m_w_masked"), sem("m_s_made"),
            sem("m_summed"), sem("m_den_made"))
        h_f_made, h_exp_made, h_ops_made, h_scan_made, h_scored, h_taken, h_summed = (
            sem("h_f_made"), sem("h_exp_made"), sem("h_ops_made"), sem("h_scan_made"), sem("h_scored"),
            sem("h_taken"), sem("h_summed"))
        n_clamped, n_squared, n_summed, n_root_made, n_recip_made, n_spread, n_applied = (
            sem("n_clamped"), sem("n_squared"), sem("n_summed"), sem("n_root_made"), sem("n_recip_made"),
            sem("n_spread"), sem("n_applied"))
        angles_made, rotated, sin_taken, cos_taken = sem("angles_made"), sem("rotated"), sem("sin_taken"), sem("cos_taken")
        lam_made, lam_summed, lam_exp = sem("lam_made"), sem("lam_summed"), sem("lam_exp")
        scores_ready, max_ready, exp_ready, norm_ready = sem("scores_ready"), sem("max_ready"), sem("exp_ready"), sem("norm_ready")
        transposed, probs_t_ready, out_ready, out_taken = sem("transposed"), sem("probs_t_ready"), sem("out_ready"), sem("out_taken")

        def col(name, layer=0, k=0):
            base, width = VCOL[name]
            return vec[:, base + layer * width + k:base + layer * width + k + 1]

        def operands(stack, layer):
            return (b_op, a_op) if stack == 1 and layer == 1 else (a_op, b_op)

        def f32(ap):
            return ap.bitcast(F32)

        def half(t, p, cols):
            return t[64 * p:64 * p + 64, cols]

        def qs(q):
            return slice(q * P, (q + 1) * P)

        def swa(layer):
            def scores(h, q, c):
                ks = slice(max(q - 1, 0) * P, (q + 1) * P)
                r = slice(64 * (h % 2), 64 * (h % 2) + 64)
                return [(y[r, T_SQ + h // 2, qs(q)], y[r, T_SK + h // 4, ks])]

            def outputs(h):
                r = slice(64 * (h % 2), 64 * (h % 2) + 64)
                vc = slice(512 + 64 * (h // 4), 576 + 64 * (h // 4))
                mm = [(qs(q), v[:, kt, vc], prob_t[:, h % 2, i, qs(q)], i == 0, i == len(kts(q)) - 1)
                      for q in range(ST) for i, kt in enumerate(kts(q))]
                return [(r, mm, o[r, 4 + h // 2, :])]

            kts = lambda q: [q - 1, q] if q else [0]
            return Attention(8, 1, 0.125, kts, scores, lambda q: band if q else band[:, P:], lambda h: (layer, h), outputs)

        def all_keys(n):
            return lambda q: list(range(n))

        def pv(h, vc, n):
            return [(slice(0, S), v[:, kt, vc], prob_t[:, h % 2, kt, :], kt == 0, kt == n - 1) for kt in range(n)]

        def dilated():
            def scores(h, q, c):
                r = slice(64 * (h % 2), 64 * (h % 2) + 64)
                return [(y[r, h // 2, qs(q)], y[r, 8 + h // 2, :])]

            def outputs(h):
                r = slice(64 * (h % 2), 64 * (h % 2) + 64)
                return [(r, pv(h, slice(64 * h, 64 * h + 64), ST), o[r, h // 2, :])]

            return Attention(16, 1, 0.125, all_keys(ST), scores, lambda q: dil[:, 384 - P * q:896 - P * q], None, outputs)

        def differential():
            def scores(h, q, c):
                r = slice(64 * c, 64 * c + 64)
                return [(y[r, h, qs(q)], y[r, 8 + h, :])]

            return Attention(8, 2, 0.125, all_keys(ST), scores, None, None,
                             lambda h: [(slice(0, P), pv(h, slice(P * h, P * h + P), ST), o[:, h, :])])

        kv_y = y[:, 8:16, :].rearrange("p t (a s) -> p (t a) s", a=2)

        def cross_attention():
            def scores(h, q, c):
                return [(y[:, 2 * h + i, qs(q)], kv_y[:, 2 * h + i, :]) for i in range(2)]

            return Attention(4, 1, 0.0625, all_keys(2), scores, None, None,
                             lambda h: [(slice(0, P), pv(h, slice(P * t, P * t + P), 2), o[:, t, :])
                                        for t in (2 * h, 2 * h + 1)])

        block = ctx.enter_context(nc.Block())

        @block.sync
        def _(sp):
            c = Counts(sp)
            for t, name in ((small[:, :], "c_small"), (vec[:, :], "vec"), (heads_c[:, :], "c_heads")):
                sp.dma_start(t, dram[name]).then_inc(loaded, 16)
            sp.dma_start(y[:, 0:2, :], dram["c_level"].rearrange("p (a b) -> p a b", a=2)).then_inc(loaded, 16)
            sp.dma_start(mem[:, :, :], dram["mem"].rearrange("p (a b) -> p a b", a=DT)).then_inc(mem_first_landed, 16)
            sp.dma_start(x[:, :, :], dram["x"].rearrange("p (a b) -> p a b", a=DT)).then_inc(x_loaded, 16)

            def load_unit(j, width):
                u = c.unit
                if c.begun(u - RAW + 1):
                    sp.wait_ge(w_hi_ready, c.by_unit(u - RAW + 1))
                if c.begun(u - RAW + 1):
                    sp.wait_ge(w_lo_ready, c.by_unit(u - RAW + 1))
                src = dram["weights"][c.pick(u, RAW), :, 0:width]
                sp.dma_start(w_raw[:, u % RAW, 0:width], src).then_inc(w_landed[u % RAW], 16)
                c.unit += 1

            runs = []
            for n, kt in STREAM:
                if runs and runs[-1][1] == kt:
                    runs[-1][0] += n
                else:
                    runs.append([n, kt])
            for n, kt in runs:
                turns = n // RAW
                if c.unit == 0:
                    for j in range(RAW):
                        load_unit(j, kt * P)
                    turns -= 1
                if turns:
                    with c.loop(turns, {}, RAW):
                        for j in range(RAW):
                            load_unit(j, kt * P)
            for k in range(DT):
                sp.wait_ge(x_ready, X_TILES - DT + k + 1)
                sp.dma_start(out[:, k * S:(k + 1) * S], x[:, k, :]).then_inc(stored, 16)
            sp.wait_ge(stored, 16 * DT)

        @block.tensor
        def _(pe):
            c = Counts(pe)
            mm = pe.matmul
            att = dict(n=0, t=0, o=0)

            def meet():
                pe.drain().then_inc(met["pe"], 1)
                pe.wait_ge(met["act"], c.count(met["act"]))
                pe.wait_ge(met["dve"], c.count(met["dve"]))
                pe.wait_ge(met["pool"], c.count(met["pool"]))

            def unit(op, kt=8, cols=S, ready=None):
                u = c.unit
                pe.wait_ge(w_lo_ready, c.by_unit(u + 1))
                if c.begun(u - 1):
                    pe.wait_ge(bank_free, c.by_unit(u - 1))
                hi, lo = op
                for k in range(kt):
                    if ready is not None:
                        pe.wait_ge(ready, c.count(ready))
                    ks = slice(k * P, (k + 1) * P)
                    for n, (w, t) in enumerate(((w_hi, hi), (w_hi, lo), (w_lo, hi))):
                        last = mm(bank[u % 2][:, 0:cols], w[:, u % SPLIT, ks], t[:, k, 0:cols],
                                  start=(k == 0 and n == 0), stop=(k == kt - 1 and n == 2))
                last.then_inc(unit_done, 1)
                c.unit += 1

            def sum_squares(cols=S):
                pe.wait_ge(sq_added, c.count(sq_added, 8))
                if c.groups > 0:
                    pe.wait_ge(root_ready, c.groups)
                c.groups += 1
                mm(bank[SUM_BANK][:, 0:cols], ones.broadcast_to([P, P]), sq_sum[:, 0:cols],
                   start=True, stop=True).then_inc(sum_ready, 1)

            def values(tiles):
                for t in tiles:
                    if att["t"] - 1 > 0:
                        pe.wait_ge(probs_t_ready, att["t"] - 1)
                    for tb in range(t.shape[-1] // P):
                        last = pe.transpose(bank[T_BANK[att["t"] % 2]][:, qs(tb)], t[:, qs(tb)], ident)
                    last.then_inc(transposed, 1)
                    att["t"] += 1

            def attention(a):
                def scores(g):
                    h, q = a.groups[g]
                    for comp in range(a.comps):
                        n = att["n"]
                        if n - 3 > 0:
                            pe.wait_ge(exp_ready, n - 3)
                        ops = a.scores(h, q, comp)
                        for i, (l, r) in enumerate(ops):
                            last = mm(bank[S_BANK[n % 4]][:, 0:r.shape[-1]], l, r,
                                      start=(i == 0), stop=(i == len(ops) - 1))
                        last.then_inc(scores_ready, 1)
                        att["n"] += 1

                def outputs(h, tiles):
                    if tiles > 0:
                        pe.wait_ge(probs_t_ready, tiles)
                    for rows, mms, _ in a.outputs(h):
                        if att["o"] - 1 > 0:
                            pe.wait_ge(out_taken, att["o"] - 1)
                        for cols, l, r, start, stop in mms:
                            last = mm(bank[O_BANK[att["o"] % 2]][rows, cols], l, r, start=start, stop=stop)
                        last.then_inc(out_ready, 1)
                        att["o"] += 1

                n0, t0 = att["n"], att["t"]
                ahead = 4 // a.comps - 1
                for g in range(ahead):
                    scores(g)
                for g, (h, q) in enumerate(a.groups):
                    if g + ahead < len(a.groups):
                        scores(g + ahead)
                    pe.wait_ge(norm_ready, c.count(norm_ready))
                    if att["t"] - 1 > 0:
                        pe.wait_ge(probs_t_ready, att["t"] - 1)
                    pr = prob[:, (n0 + g * a.comps) % 4, :]
                    for i in range(len(a.key_tiles(q))):
                        last = pe.transpose(bank[T_BANK[att["t"] % 2]][:, qs(i)], pr[:, qs(i)], ident)
                    last.then_inc(transposed, 1)
                    att["t"] += 1
                    if q == 0 and h > 0:
                        outputs(h - 1, t0 + g)
                outputs(a.heads - 1, att["t"])

            def head_norm(tiles, rows, window, spread):
                pe.wait_ge(n_squared, c.since(n_squared, tiles))
                for j in range(tiles):
                    last = mm(bank[5][0:rows, :], window(j), n_sq[:, j, :], start=(j == 0), stop=(j == tiles - 1))
                last.then_inc(n_summed, 1)
                pe.wait_ge(n_recip_made, c.since(n_recip_made, 1))
                for j in range(tiles):
                    if j - 1 > 0:
                        pe.wait_ge(n_applied, c.since(n_applied, j - 1))
                    mm(bank[6 + j % 2][:, :], spread(j), n_row[0:rows, 1, :], start=True, stop=True).then_inc(n_spread, 1)
                c.add(n_squared, tiles)
                c.add(n_recip_made, 1)
                c.add(n_applied, tiles)
                meet()

            def head_norm64(tiles):
                head_norm(tiles, 2 * tiles, lambda j: halves[:, 10 - 2 * j:10 - 2 * j + 2 * tiles],
                          lambda j: heads_c[0:2 * tiles, qs(j)])

            def rope(tiles):
                for j, t in enumerate(tiles):
                    if j - 1 > 0:
                        pe.wait_ge(sin_taken, c.since(sin_taken, j - 1))
                    mm(bank[j % 2][:, :], rot, y[:, t, :], start=True, stop=True).then_inc(rotated, 1)
                c.add(sin_taken, len(tiles))

            def load(l):
                sum_squares(MEM)
                pe.wait_ge(lam_made, c.count(lam_made))
                mm(bank[3][:, 0:2], ones.broadcast_to([P, P]), lam_e, start=True, stop=True).then_inc(lam_summed, 1)

            def wide(stack, l):
                op = operands(stack, l)[0]
                unit(op, ready=a_ready)
                sum_squares()
                for _ in range(3):
                    unit(op)
                with c.loop(WIN_T // 4 - 1, {}, 4):
                    for _ in range(4):
                        unit(op)

            def mlstm():
                for tb in range(ST):
                    mm(bank[5][:, 4 * tb:4 * tb + 4], m_row[0:4, 3, qs(tb)], ident[0:4, 0:4], start=True, stop=True)
                for p in range(2):
                    last = mm(bank[6 + p][:, :], heads_c[0:4, qs(p)], m_row[0:4, 5, :], start=True, stop=True)
                last.then_inc(cols_made, 1)
                meet()
                blocks = [(h, j) for h in range(4) for j in range(ST)]

                def scores(n):
                    h, j = blocks[n]
                    r = slice(64 * (h % 2), 64 * (h % 2) + 64)
                    if j == 0:
                        if 4 * (h - 1) > 0:
                            pe.wait_ge(m_gap_made, c.since(m_gap_made, 4 * (h - 1)))
                        mm(bank[2 + h % 2][:, :], heads_c[0:4, 64 * h:64 * h + 1].broadcast_to([4, P]),
                           m_row[0:4, 4, :], start=True, stop=True)
                    if n - 1 > 0:
                        pe.wait_ge(m_s_made, c.since(m_s_made, n - 1))
                    mm(bank[n % 2][:, j * P:], y[r, T_MK + h // 2, qs(j)], y[r, T_MQ + h // 2, j * P:],
                       start=True, stop=True).then_inc(m_scored, 1)

                scores(0)
                for n, (h, j) in enumerate(blocks):
                    if n + 1 < len(blocks):
                        scores(n + 1)
                    pe.wait_ge(m_s_made, c.since(m_s_made, n + 1))
                    r = slice(64 * (h % 2), 64 * (h % 2) + 64)
                    w = m_s[:, n % 2, j * P:]
                    num, den = bank[6 - 2 * (h // 2)], bank[7 - 2 * (h // 2)]
                    mm(num[r, j * P:], v[:, j, 64 * h:64 * h + 64], w, start=(j == 0), stop=(j == 3))
                    mm(den[r, j * P:], ones.broadcast_to([P, 64]), w, start=(j == 0), stop=(j == 3)).then_inc(m_summed, 1)
                c.add(m_gap_made, 16)
                c.add(m_s_made, 16)
                meet()

            def hgrn():
                meet()
                for lev in range(10):
                    if lev < 9:
                        pe.wait_ge(h_ops_made, c.since(h_ops_made, lev + 1))
                    for h in range(4):
                        n = 4 * lev + h
                        r = slice(64 * (h % 2), 64 * (h % 2) + 64)
                        if lev < 9:
                            q_, k_ = h_q[r, lev % 2, h // 2, :], h_k[r, lev % 2, h // 2, :]
                        else:
                            q_, k_ = y[r, T_HQ + h // 2, :], h_key[r, h // 2, :]
                        if n - 3 > 0:
                            pe.wait_ge(h_taken, c.since(h_taken, n - 3))
                        if lev == 7:
                            pairs = [(qs(0), qs(0), qs(1)), (qs(1), qs(2), qs(3))]
                        elif lev == 8:
                            late = slice(2 * P, 4 * P)
                            pairs = [(slice(0, 2 * P), qs(0), late), (late, qs(1), late)]
                        else:
                            pairs = [(qs(i), qs(i), qs(i)) for i in range(ST)]
                        for cols, ks, ls in pairs:
                            last = mm(bank[n % 4][:, cols], k_[:, ks], q_[:, ls], start=True, stop=True)
                        last.then_inc(h_scored, 1)
                c.add(h_ops_made, 9)
                pe.wait_ge(h_taken, c.since(h_taken, 40))
                c.add(h_taken, 40)
                late = slice(2 * P, 4 * P)
                for h in range(4):
                    r = slice(64 * (h % 2), 64 * (h % 2) + 64)
                    vc = slice(256 + 64 * h, 320 + 64 * h)
                    terms = [(qs(i), i, h_d[:, h, i, :]) for i in range(ST)]
                    terms += [(qs(1), 0, h_o1[:, h, 0, :]), (qs(3), 2, h_o1[:, h, 1, :]),
                              (late, 0, h_o2[:, h, 0, :]), (late, 1, h_o2[:, h, 1, :])]
                    for i, (cols, kt, rhs) in enumerate(terms):
                        last = mm(bank[6 + h // 2][r, cols], v[:, kt, vc], rhs, start=(i == 0),
                                  stop=(i == len(terms) - 1), skip_group_check=True)
                last.then_inc(h_summed, 1)
                meet()

            def mix1(l):
                meet()
                values([y[:, t, :] for t in range(T_MV, T_SV + 1)])
                meet()
                mlstm()
                hgrn()
                head_norm64(4)
                head_norm64(6)
                rope(range(T_SQ, T_SK + 2))
                meet()
                attention(swa(l))
                meet()

            def out_product(stack, l):
                h = operands(stack, l)[1]
                unit(h, ready=h_ready)
                for _ in range(7):
                    unit(h)

            def ffn1(l):
                a, h = operands(1, l)

                def chunk(first=False):
                    for j in range(8):
                        unit(a, ready=a_ready if first and j == 0 else None)
                        if first and j == 0:
                            sum_squares()
                    for j in range(8):
                        unit(h, ready=h_ready if j == 0 else None)

                chunk(True)
                with c.loop(FFN1_CHUNKS - 2, {h_ready: 8}, 16):
                    chunk()
                chunk()

            def proj(l):
                h = operands(1, l)[1]
                pe.wait_ge(h_ready, c.count(h_ready, 2))
                for j in range(8):
                    unit(h, kt=2)
                    if j == 0:
                        sum_squares()

            def gate(l):
                a = operands(1, l)[0]
                unit(a, ready=a_ready)
                unit(a)
                sum_squares()
                for _ in range(6):
                    unit(a)

            def mix2(l):
                meet()
                if l == 0:
                    meet()
                rope(range(16))
                values([y[:, 16 + t, :] for t in range(8)])
                meet()
                attention(dilated() if l == 0 else differential())
                meet()
                if l == 1:
                    head_norm(8, 8, lambda j: unit8[:, 7 - j:15 - j], lambda j: ident[0:8, j:j + 1].broadcast_to([8, P]))

            def kv(l):
                h = operands(2, l)[1]
                unit(h, cols=MEM, ready=h_ready)
                for _ in range(3):
                    unit(h, cols=MEM)
                with c.loop(3, {}, 4):
                    for _ in range(4):
                        unit(h, cols=MEM)

            def xq(l):
                a = operands(2, l)[0]
                unit(a, ready=a_ready)
                sum_squares()
                for _ in range(7):
                    unit(a)

            def cross(l):
                meet()
                values([kv_y[:, 8 + t, :] for t in range(8)])
                meet()
                attention(cross_attention())
                meet()

            def ffn2(l):
                a, h = operands(2, l)
                pe.wait_ge(a_ready, c.count(a_ready, 8))
                sum_squares()

                def chunk(tiles):
                    for _ in range(2 * tiles):
                        unit(a)
                    pe.wait_ge(h_ready, c.count(h_ready, tiles))
                    for _ in range(8):
                        unit(h, kt=tiles)

                with c.loop(2, {h_ready: 8}, 24):
                    chunk(8)
                chunk(6)
                sum_squares()

            def out2(l):
                out_product(2, l)
                sum_squares()

            load(0)
            for l in range(LAYERS):
                wide(1, l)
                mix1(l)
                out_product(1, l)
                ffn1(l)
                proj(l)
                gate(l)
            for l in range(LAYERS):
                wide(2, l)
                mix2(l)
                out2(l)
                kv(l)
                xq(l)
                cross(l)
                out2(l)
                ffn2(l)

        @block.scalar
        def _(act):
            c = Counts(act)
            f = act.activation
            att = dict(n=0, t=0, o=0, group=[], outs=[])

            def meet():
                act.drain().then_inc(met["act"], 1)
                act.wait_ge(met["pe"], c.count(met["pe"]))
                act.wait_ge(met["dve"], c.count(met["dve"]))
                act.wait_ge(met["pool"], c.count(met["pool"]))

            widths = [kt * P for n, kt in STREAM for _ in range(n)]

            def split_hi():
                u = c.next
                if u == UNITS:
                    return
                act.wait_ge(w_landed[u % RAW], c.by_unit(16 * (u // RAW + 1), 4))
                if c.begun(u - 1):
                    act.wait_ge(unit_done, c.by_unit(u - 1))
                f(w_hi[:, u % SPLIT, 0:widths[u]], w_raw[:, u % RAW, 0:widths[u]], ACT.Copy).then_inc(w_hi_ready, 1)
                c.next += 1

            def step(work=None, before=None):
                split_hi()
                if before is not None:
                    before()
                if work is not None:
                    work(c.unit)
                c.unit += 1

            def taken(u):
                act.wait_ge(bank_free, c.by_unit(u + 1))

            def square(src, cols=S):
                n = c.squares
                if n - 1 > 0:
                    act.wait_ge(sq_added, n - 1)
                f(sq[:, n % 2, 0:cols], src, ACT.Square).then_inc(sq_ready, 1)
                c.squares += 1

            def root_of_mean(cols=S):
                act.wait_ge(sum_ready, c.count(sum_ready))
                if c.groups > 0:
                    act.wait_ge(recip_ready, c.groups)
                c.groups += 1
                f(root[:, 0:cols], bank[SUM_BANK][:, 0:cols], ACT.Sqrt, bias=eps, scale=1.0 / D).then_inc(root_ready, 1)

            def round_x(dst, k, gain, wait=True):
                if wait:
                    act.wait_ge(x_ready, c.count(x_ready))
                f(dst[0][:, k, :], x[:, k, :], ACT.Copy, scale=gain).then_inc(a_hi_ready, 1)
                square(x[:, k, :])

            def values(n, tok=ST):
                for i in range(n):
                    act.wait_ge(transposed, c.count(transposed))
                    f(v[:, 0:tok, qs(i)], bank[T_BANK[att["t"] % 2]][:, 0:tok * P].rearrange("p (a b) -> p a b", a=tok),
                      ACT.Copy).then_inc(probs_t_ready, 1)
                    att["t"] += 1

            def attention(a):
                def exps(g):
                    h, q = a.groups[g]
                    nk = P * len(a.key_tiles(q))
                    for comp in range(a.comps):
                        n = att["n"]
                        s = n % 8
                        act.wait_ge(max_ready, c.count(max_ready))
                        if n >= 4:
                            if att["group"][n - 4] + 1 > 0:
                                act.wait_ge(transposed, att["group"][n - 4] + 1)
                        last = f(prob[:, n % 4, 0:nk], bank[S_BANK[n % 4]][:, 0:nk], ACT.Exp, bias=stat_n[:, s:s + 1],
                                 scale=a.scale, accum_out=stat_d[:, s:s + 1])
                        if a.sink is not None:
                            last = f(stat_s[:, s:s + 1], col("sinks", *a.sink(h)), ACT.Exp, bias=stat_n[:, s:s + 1])
                        last.then_inc(exp_ready, 1)
                        att["group"].append(att["t0"] + g)
                        att["n"] += 1

                att["t0"] = att["t"]
                exps(0)
                for g, (h, q) in enumerate(a.groups):
                    if g + 1 < len(a.groups):
                        exps(g + 1)
                    act.wait_ge(transposed, c.count(transposed))
                    if q == 0 and len(att["outs"]) >= 2:
                        if att["outs"][-2] > 0:
                            act.wait_ge(out_ready, att["outs"][-2])
                    nk = len(a.key_tiles(q))
                    f(prob_t[:, h % 2, 0:nk, qs(q)],
                      bank[T_BANK[att["t"] % 2]][:, 0:nk * P].rearrange("p (a b) -> p a b", a=nk),
                      ACT.Copy).then_inc(probs_t_ready, 1)
                    att["t"] += 1
                    if q == ST - 1:
                        att["o"] += len(a.outputs(h))
                        att["outs"].append(att["o"])

            def head_norm(tiles, rows, src, scale=1.0, width=64, bias=None, clamped=False):
                for j in range(tiles):
                    if clamped:
                        act.wait_ge(n_clamped, c.since(n_clamped, j + 1))
                    f(n_sq[:, j, :], src(j), ACT.Square, scale=scale).then_inc(n_squared, 1)
                c.add(n_clamped, tiles if clamped else 0)
                act.wait_ge(n_summed, c.count(n_summed))
                f(n_row[0:rows, 0, :], bank[5][0:rows, :], ACT.Sqrt, bias=(eps if bias is None else bias)[0:rows, :],
                  scale=1.0 / width).then_inc(n_root_made, 1)
                meet()

            def load(l):
                act.wait_ge(loaded, 64)
                act.wait_ge(mem_first_landed, 16)
                act.wait_ge(lam_made, c.count(lam_made))
                for k in range(DT):
                    square(mem[:, k, :], MEM)
                root_of_mean(MEM)
                act.wait_ge(lam_summed, c.count(lam_summed))
                f(lam_e, bank[3][:, 0:2], ACT.Exp).then_inc(lam_exp, 1)
                f(lb[:, 2:4], lb[:, 0:2], ACT.Sigmoid)
                f(one_lb[:, 2:4], lb[:, 0:2], ACT.Sigmoid, scale=-1.0)
                act.drain()
                f(lb[:, 0:2], lb[:, 0:2], ACT.Copy, scale=0.0).then_inc(lam_exp, 1)
                act.wait_ge(x_loaded, 16)
                for k in range(DT):
                    round_x(a_op, k, col("in_g", 0, k), wait=False)
                split_hi()

            def wide(stack, l):
                def bias(u):
                    taken(u)
                    t = c.pick(u - first, 4)
                    b = VCOL["b_in"][0] + l * WIN_T
                    f(y[:, t, :], y[:, t, :], ACT.Identity, bias=vec[:, bass.ds(t + b, 1)])

                first = c.unit
                work = bias if stack == 1 else None
                step(work, before=root_of_mean)
                for _ in range(3):
                    step(work)
                with c.loop(WIN_T // 4 - 1, {}, 4):
                    for _ in range(4):
                        step(work)

            def tables():
                act.wait_ge(angles_made, c.count(angles_made))
                f(sin_t[:, :], ang[:, 0, :], ACT.Sin)
                f(cos_t[:, :], ang[:, 2, :], ACT.Sin, bias=half_pi, scale=-1.0)

            def mlstm():
                act.wait_ge(cols_made, c.count(cols_made))
                f(m_col[:, :], bank[5][:, 0:16], ACT.Copy)
                for p in range(2):
                    f(m_end[:, p, :], bank[6 + p][:, :], ACT.Copy)
                meet()
                for n in range(16):
                    j = n % 4
                    act.wait_ge(m_gap_made, c.since(m_gap_made, n + 1))
                    if n - 1 > 0:
                        act.wait_ge(m_s_made, c.since(m_s_made, n - 1))
                    f(m_w[:, n % 2, j * P:], m_t[:, n % 2, j * P:], ACT.Exp, scale=-1.0).then_inc(m_w_made, 1)
                c.add(m_gap_made, 16)
                c.add(m_s_made, 16)
                act.wait_ge(m_summed, c.count(m_summed, 16))
                for p in range(2):
                    f(m_den[:, p, :], bank[7 - 2 * p][:, :], ACT.Abs).then_inc(m_den_made, 1)
                meet()

            def hgrn():
                act.wait_ge(h_f_made, c.count(h_f_made))
                f(h_lp[:, :, :], y[:, T_HF:T_HF + 2, :], ACT.Ln)
                meet()
                for lev in range(9):
                    if 4 * (lev - 1) > 0:
                        act.wait_ge(h_scored, c.since(h_scored, 4 * (lev - 1)))
                    if lev > 0:
                        act.wait_ge(h_scan_made, c.since(h_scan_made, lev))
                    f(h_q[:, lev % 2, :, :], h_lp[:, :, :], ACT.Exp)
                    f(h_k[:, lev % 2, :, :], h_ls[:, :, :], ACT.Exp).then_inc(h_exp_made, 1)
                c.add(h_scored, 40)
                c.add(h_scan_made, 8)
                act.wait_ge(h_summed, c.count(h_summed))
                for p in range(2):
                    f(o[:, 2 + p, :], bank[6 + p][:, :], ACT.Copy)
                meet()

            def mix1(l):
                meet()
                if l == 0:
                    tables()
                values(5)
                act.wait_ge(gates_split, c.count(gates_split))
                f(m_row[0:4, 2, :], m_row[0:4, 2, :], ACT.Exp)
                act.drain()
                f(m_row[0:4, 2, :], m_row[0:4, 2, :], ACT.Ln, bias=ones[0:4, :]).then_inc(gates_log, 1)
                f(y[:, T_MO:T_MO + 2, :], y[:, T_MO:T_MO + 2, :], ACT.Sigmoid)
                f(h_neg[:, :, :], y[:, T_HF:T_HF + 2, :], ACT.Sigmoid, scale=-1.0)
                f(y[:, T_HF:T_HF + 2, :], y[:, T_HF:T_HF + 2, :], ACT.Sigmoid)
                f(y[:, T_HQ:T_HQ + 2, :], y[:, T_HQ:T_HQ + 2, :], ACT.Silu)
                f(y[:, T_HG:T_HG + 2, :], y[:, T_HG:T_HG + 2, :], ACT.Silu)
                for t in range(4):
                    act.wait_ge(conv_made, c.count(conv_made))
                    f(y[:, T_MQ + t, :], o[:, t, :], ACT.Silu)
                act.wait_ge(gates_made, c.count(gates_made))
                f(m_row[0:4, 5, :], m_row[0:4, 5, :], ACT.Exp)
                meet()
                mlstm()
                hgrn()
                head_norm(4, 8, lambda j: o[:, j, :])
                head_norm(6, 12, lambda j: y[:, T_SQ + j, :])
                meet()
                attention(swa(l))
                meet()

            def round_o(stack, l):
                h = operands(stack, l)[1]
                for k in range(DT):
                    f(h[0][:, k, :], o[:, k, :], ACT.Copy).then_inc(h_hi_ready, 1)

            def out1(l):
                a = operands(1, l)[0]
                round_o(1, l)
                for k in range(8):
                    step(lambda u: round_x(a, k, col("mlp_g", l, k)))

            def ffn1(l):
                a, h = operands(1, l)

                def chunk(first=False, last=False):
                    for j in range(8):
                        def hidden(u):
                            taken(u)
                            f(y[:, 20 + j % 2, :], y[:, 16 + j % 2, :], ACT.Square)
                            f(h[0][:, j, :], y[:, 16 + j % 2, :], ACT.Square).then_inc(h_hi_ready, 1)

                        step(hidden, before=root_of_mean if first and j == 0 else None)
                    for k in range(8):
                        step((lambda u: round_x(a, k, col("ple_g", l, k))) if last else None)

                chunk(first=True)
                with c.loop(FFN1_CHUNKS - 2, {}, 16):
                    chunk()
                chunk(last=True)

            def proj(l):
                h = operands(1, l)[1]
                act.wait_ge(ple_landed, c.count(ple_landed, 16))
                for k in range(2):
                    f(h[0][:, k, :], ple[:, k, :], ACT.Copy).then_inc(h_hi_ready, 1)
                for k in range(8):
                    def squares(u):
                        taken(u)
                        square(y[:, 8 + k, :])

                    step(squares, before=root_of_mean if k == 0 else None)

            def gate(l):
                h = operands(1, l)[1]
                for k in range(8):
                    def sigmoid(u):
                        taken(u)
                        f(y[:, k, :], y[:, k, :], ACT.Sigmoid).then_inc(act_made, 1)

                    step(sigmoid)
                    if k == 1:
                        root_of_mean()
                    if k >= 2:
                        round_x(h, k - 2, next_gain(l, k - 2))
                for k in (6, 7):
                    round_x(h, k, next_gain(l, k))

            def next_gain(l, k):
                return col("in_g", l + 1, k) if l + 1 < LAYERS else col("mix_pre", 0, k)

            def out2(l, name):
                round_o(2, l)
                for k in range(8):
                    def squares(u):
                        taken(u)
                        square(y[:, k, :])

                    step(squares)
                post(l, name)

            def post(l, name):
                root_of_mean()
                for k in range(8):
                    if name is not None:
                        round_x(a_op, k, col(name[0], name[1], k))

            def mix2(l):
                meet()
                if l == 0:
                    tables()
                    meet()
                values(8)
                meet()
                attention(dilated() if l == 0 else differential())
                meet()
                if l == 1:
                    head_norm(8, 8, lambda j: n_sq[:, j, :], 2.0 ** -32, P, eps_big, clamped=True)

            def kv(l):
                h = operands(2, l)[1]
                act.wait_ge(mem_landed, c.count(mem_landed, 16))
                for k in range(DT):
                    f(h[0][:, k, 0:MEM], mem[:, k, :], ACT.Copy, scale=col("mem_kv", l, k)).then_inc(h_hi_ready, 1)
                for _ in range(4):
                    step()
                with c.loop(3, {}, 4):
                    for _ in range(4):
                        step()

            def xq(l):
                step()
                root_of_mean()
                for _ in range(7):
                    step()

            def cross(l):
                meet()
                values(8, 2)
                meet()
                attention(cross_attention())
                meet()

            def ffn2(l):
                h = operands(2, l)[1]
                root_of_mean()

                def chunk(tiles, last=False):
                    for j in range(tiles):
                        def silu(u):
                            taken(u)
                            f(y[:, 19, :], y[:, 16, :], ACT.Silu).then_inc(act_made, 1)

                        def hidden(u):
                            act.wait_ge(f_ready, c.count(f_ready))
                            f(h[0][:, j, :], y[:, 20 + j % 2, :], ACT.Copy).then_inc(h_hi_ready, 1)

                        step(silu)
                        step(hidden)
                    for k in range(8):
                        def squares(u):
                            taken(u)
                            square(y[:, k, :])

                        step(squares if last else None)

                with c.loop(2, {f_ready: 8}, 24):
                    chunk(8)
                chunk(6, last=True)
                post(l, ("mix_pre", l + 1) if l + 1 < LAYERS else None)

            load(0)
            for l in range(LAYERS):
                wide(1, l)
                mix1(l)
                out1(l)
                ffn1(l)
                proj(l)
                gate(l)
            for l in range(LAYERS):
                wide(2, l)
                mix2(l)
                out2(l, ("mem_pre", l))
                kv(l)
                xq(l)
                cross(l)
                out2(l, ("ffn_pre", l))
                ffn2(l)

        @block.vector
        def _(dve):
            c = Counts(dve)
            tt, ts, stt = dve.tensor_tensor, dve.tensor_scalar, dve.scalar_tensor_tensor
            att = dict(n=0, o=0)
            widths = [kt * P for n, kt in STREAM for _ in range(n)]

            def meet():
                dve.drain().then_inc(met["dve"], 1)
                dve.wait_ge(met["pe"], c.count(met["pe"]))
                dve.wait_ge(met["act"], c.count(met["act"]))
                dve.wait_ge(met["pool"], c.count(met["pool"]))

            def split_lo():
                u = c.next
                if u == UNITS:
                    return
                dve.wait_ge(w_hi_ready, c.by_unit(u + 1))
                w = slice(0, widths[u])
                tt(w_lo[:, u % SPLIT, w], w_raw[:, u % RAW, w], f32(w_hi[:, u % SPLIT, w]), ALU.subtract).then_inc(w_lo_ready, 1)
                c.next += 1

            def step(work):
                split_lo()
                u = c.unit
                dve.wait_ge(unit_done, c.by_unit(u + 1))
                work(u, bank[u % 2])
                c.unit += 1

            def recip(dst, cols=S):
                dve.wait_ge(root_ready, c.count(root_ready))
                dve.reciprocal(dst[:, 0:cols], root[:, 0:cols]).then_inc(recip_ready, 1)
                dve.drain()

            def lo_x(dst, k, gain):
                dve.wait_ge(a_hi_ready, c.count(a_hi_ready))
                stt(dst[1][:, k, :], x[:, k, :], gain, f32(dst[0][:, k, :]), ALU.mult, ALU.subtract).then_inc(a_ready, 1)

            def lo_h(h, k, src):
                dve.wait_ge(h_hi_ready, c.count(h_hi_ready))
                tt(h[1][:, k, :], src, f32(h[0][:, k, :]), ALU.subtract).then_inc(h_ready, 1)

            def next_gain(l, k):
                return col("in_g", l + 1, k) if l + 1 < LAYERS else col("mix_pre", 0, k)

            def attention(a):
                def maxima(g):
                    h, q = a.groups[g]
                    nk = P * len(a.key_tiles(q))
                    for _ in range(a.comps):
                        n = att["n"]
                        b, s = bank[S_BANK[n % 4]][:, 0:nk], stat_n[:, n % 8:n % 8 + 1]
                        dve.wait_ge(scores_ready, c.count(scores_ready))
                        if a.mask is not None:
                            dve.tensor_tensor_reduce(out=b, in0=b, in1=a.mask(q), scale=1.0, scalar=-3e38,
                                                     op0=ALU.add, op1=ALU.max, accum_out=s)
                        else:
                            dve.reduce_max(s, b, mybir.AxisListType.X)
                        dve.drain()
                        if a.sink is not None:
                            l, hh = a.sink(h)
                            ts(s, s, -a.scale, neg_sink[:, 8 * l + hh:8 * l + hh + 1], ALU.mult, ALU.min).then_inc(max_ready, 1)
                        else:
                            ts(s, s, -a.scale, None, ALU.mult).then_inc(max_ready, 1)
                        att["n"] += 1

                def normalise(g):
                    h, q = a.groups[g]
                    nk = P * len(a.key_tiles(q))
                    dve.wait_ge(exp_ready, c.count(exp_ready, a.comps))
                    ns = [n0 + g * a.comps + i for i in range(a.comps)]
                    for n in ns:
                        d = stat_d[:, n % 8:n % 8 + 1]
                        if a.sink is not None:
                            tt(d, d, stat_s[:, n % 8:n % 8 + 1], ALU.add)
                            dve.drain()
                        dve.reciprocal(d, d)
                    dve.drain()
                    p0, d0 = prob[:, ns[0] % 4, 0:nk], stat_d[:, ns[0] % 8:ns[0] % 8 + 1]
                    if a.comps == 1:
                        ts(p0, p0, d0, None, ALU.mult).then_inc(norm_ready, 1)
                    else:
                        p1, d1 = prob[:, ns[1] % 4, 0:nk], stat_d[:, ns[1] % 8:ns[1] % 8 + 1]
                        ts(p1, p1, d1, lam, ALU.mult, ALU.mult)
                        dve.drain()
                        stt(p0, p0, d0, p1, ALU.mult, ALU.subtract).then_inc(norm_ready, 1)

                def take(h):
                    for rows, _, dst in a.outputs(h):
                        dve.wait_ge(out_ready, c.count(out_ready))
                        dve.tensor_copy(dst, bank[O_BANK[att["o"] % 2]][rows, :]).then_inc(out_taken, 1)
                        att["o"] += 1

                n0 = att["n"]
                ahead = 2 // a.comps
                for g in range(ahead):
                    maxima(g)
                for g, (h, q) in enumerate(a.groups):
                    normalise(g)
                    if g + ahead < len(a.groups):
                        maxima(g + ahead)
                    if q == 1 and h > 0:
                        take(h - 1)
                take(a.heads - 1)

            def head_norm(tiles, rows, apply):
                dve.wait_ge(n_root_made, c.count(n_root_made))
                dve.reciprocal(n_row[0:rows, 1, :], n_row[0:rows, 0, :])
                dve.drain().then_inc(n_recip_made, 1)
                for j in range(tiles):
                    dve.wait_ge(n_spread, c.count(n_spread))
                    apply(j, bank[6 + j % 2])
                meet()

            def rope(tiles):
                for j, t in enumerate(tiles):
                    dve.wait_ge(rotated, c.since(rotated, j + 1))
                    tt(r_t[:, j % 2, :], bank[j % 2][:, :], sin_t[:, :], ALU.mult).then_inc(sin_taken, 1)
                    dve.drain()
                    dve.wait_ge(cos_taken, c.since(cos_taken, j + 1))
                    tt(y[:, t, :], y[:, t, :], r_t[:, j % 2, :], ALU.add)
                c.add(rotated, len(tiles))
                c.add(cos_taken, len(tiles))

            def load(l):
                dve.memset(eps, EPS)
                dve.memset(eps_big, EPS * 2.0 ** -64)
                dve.memset(half_pi, float(np.pi / 2))
                dve.memset(ones, 1.0)
                dve.memset(one_lb[:, 0:2], 1.0)
                dve.wait_ge(loaded, 64)
                dve.tensor_copy(level[:, :, :].rearrange("p a b -> p (a b)"), y[:, 0:2, :].rearrange("p a b -> p (a b)"))
                b = VCOL["lb_logit"][0]
                tt(lb[:, 0:2], vec[:, b + 2:b + 4], vec[:, b:b + 2], ALU.subtract)
                b = VCOL["sinks"][0]
                ts(neg_sink, vec[:, b:b + 16], -1.0, None, ALU.mult)
                b = VCOL["lam"][0]
                tt(lam_e, vec[:, b:b + 2], vec[:, b + 2:b + 4], ALU.mult)
                dve.drain().then_inc(lam_made, 1)
                dve.wait_ge(lam_exp, c.count(lam_exp, 2))
                ts(lam, lam_e[:, 0:1], lam_e[:, 1:2], float(0.8 - 0.6 * np.exp(-0.3)), ALU.subtract, ALU.add)
                recip(r_mem, MEM)
                dve.wait_ge(x_loaded, 16)
                for k in range(DT):
                    lo_x(a_op, k, col("in_g", 0, k))
                split_lo()

            def wide(stack, l):
                def scaled(u, b):
                    t = c.pick(u - first, 4)
                    tt(y[:, t, :], b[:, :], r_x[:, :], ALU.mult).then_inc(bank_free, 1)

                first = c.unit
                recip(r_x)
                for _ in range(4):
                    step(scaled)
                with c.loop(WIN_T // 4 - 1, {}, 4):
                    for _ in range(4):
                        step(scaled)

            def tables():
                dve.wait_ge(pos_landed, c.count(pos_landed, 16))
                r, t, n = ang[:, 0, :], ang[:, 1, :], ang[:, 2, :]
                dve.tensor_copy(t, pos_i[:, :])
                dve.drain()
                ts(r, t, col("inv_freq"), None, ALU.mult)
                dve.drain()
                ts(t, r, float(1 / _TWO_PI), MAGIC, ALU.mult, ALU.add)
                dve.drain()
                ts(t, t, MAGIC, None, ALU.subtract)
                dve.drain()
                for part in (C1, C2, C3):
                    stt(r, t, -part, r, ALU.mult, ALU.add)
                    dve.drain()
                ts(r, r, 3.1415925, -3.1415925, ALU.min, ALU.max)
                dve.drain()
                stt(n, r, -1.0, r, ALU.mult, ALU.max)
                dve.drain().then_inc(angles_made, 1)

            def gates_first(l):
                g = y[32:36, T_GATE, :]
                b = VCOL["f_b"][0] + l
                ts(m_row[0:4, 0, :], g, vec[32:36, b:b + 1], None, ALU.add)
                dve.drain()
                ts(m_row[0:4, 1, :], m_row[0:4, 0, :], 0.0, None, ALU.min)
                stt(m_row[0:4, 2, :], m_row[0:4, 0, :], -1.0, m_row[0:4, 0, :], ALU.mult, ALU.min)
                dve.memset(m_row[0:4, 7, :], 0.0)
                dve.drain().then_inc(gates_split, 1)

            def gates_second():
                row = lambda i: m_row[0:4, i, :]
                dve.wait_ge(gates_log, c.count(gates_log))
                tt(row(0), row(1), row(2), ALU.subtract)
                dve.drain()
                dve.tensor_tensor_scan(row(6), row(0), row(7), 0.0, ALU.add, ALU.add)
                dve.drain()
                tt(row(3), y[0:4, T_GATE, :], row(6), ALU.subtract)
                dve.drain()
                dve.tensor_tensor_scan(row(4), row(3), row(3), 0.0, ALU.max, ALU.max)
                dve.drain()
                tt(row(5), row(6), row(4), ALU.add)
                dve.drain()
                ts(row(5), row(5), -1.0, 88.0, ALU.mult, ALU.min)
                dve.drain().then_inc(gates_made, 1)

            def conv(l, t):
                w = lambda j: col("conv_w", l, 4 * j + t)
                u, acc = y[:, T_MQ + t, :], o[:, t, :]
                ts(acc, u, w(3), col("conv_b", l, t), ALU.mult, ALU.add)
                for back in (1, 2, 3):
                    dve.drain()
                    last = stt(acc[:, back:], u[:, :S - back], w(3 - back), acc[:, back:], ALU.mult, ALU.add)
                last.then_inc(conv_made, 1)

            def mlstm():
                meet()

                def gap(n):
                    h, j = n // 4, n % 4
                    dve.wait_ge(m_scored, c.since(m_scored, n + 1))
                    if n - 1 > 0:
                        dve.wait_ge(m_w_made, c.since(m_w_made, n - 1))
                    ts(m_t[:, n % 2, j * P:], bank[2 + h % 2][:, j * P:], m_col[:, 4 * j + h:4 * j + h + 1], 0.0,
                       ALU.subtract, ALU.max).then_inc(m_gap_made, 1)

                gap(0)
                for n in range(16):
                    j = n % 4
                    if n + 1 < 16:
                        gap(n + 1)
                    dve.wait_ge(m_w_masked, c.since(m_w_masked, n + 1))
                    if n - 1 > 0:
                        dve.wait_ge(m_summed, c.since(m_summed, n - 1))
                    stt(m_s[:, n % 2, j * P:], bank[n % 2][:, j * P:], 0.125, m_w[:, n % 2, j * P:],
                        ALU.mult, ALU.mult).then_inc(m_s_made, 1)
                c.add(m_scored, 16)
                c.add(m_w_made, 16)
                c.add(m_w_masked, 16)
                c.add(m_summed, 16)
                for p in range(2):
                    dve.wait_ge(m_den_made, c.count(m_den_made))
                    tt(m_den[:, p, :], m_den[:, p, :], m_end[:, p, :], ALU.max)
                    dve.drain()
                    dve.reciprocal(m_rec[:, p, :], m_den[:, p, :])
                    dve.drain()
                    tt(o[:, p, :], bank[6 - 2 * p][:, :], m_rec[:, p, :], ALU.mult)
                meet()

            def hgrn(l):
                for t in range(2):
                    k = 2 * l + t
                    ts(h_key[:, t, :], h_neg[:, t, :], one_lb[:, k:k + 1], None, ALU.mult)
                    ts(y[:, T_HF + t, :], y[:, T_HF + t, :], one_lb[:, k:k + 1], lb[:, k:k + 1], ALU.mult, ALU.add)
                dve.drain()
                last = ts(y[:, T_HF:T_HF + 2, :], y[:, T_HF:T_HF + 2, :], 2.0 ** -63, None, ALU.max)
                last.then_inc(h_f_made, 1)
                meet()

                def take(lev):
                    for h in range(4):
                        n = 4 * lev + h
                        dve.wait_ge(h_scored, c.since(h_scored, n + 1))
                        b = bank[n % 4]
                        if lev == 7:
                            last = dve.tensor_copy(h_o1[:, h, :, :], b[:, 0:2 * P].rearrange("p (a b) -> p a b", a=2))
                        elif lev == 8:
                            last = dve.tensor_copy(h_o2[:, h, :, :], b[:, :].rearrange("p (a b) -> p a b", a=2))
                        else:
                            m = level[:, min(lev, 7), :].unsqueeze(1).broadcast_to([P, ST, P])
                            last = dve.copy_predicated(h_d[:, h, :, :], m, b[:, :].rearrange("p (a b) -> p a b", a=ST))
                        last.then_inc(h_taken, 1)

                for lev in range(10):
                    if lev < 9:
                        w = 2 ** lev
                        b = lev % 2
                        dve.wait_ge(h_exp_made, c.since(h_exp_made, lev + 1))
                        tt(h_q[:, b, :, :], h_q[:, b, :, :], y[:, T_HQ:T_HQ + 2, :], ALU.mult)
                        tt(h_k[:, b, :, :], h_k[:, b, :, :], h_key[:, :, :], ALU.mult).then_inc(h_ops_made, 1)
                        if lev < 8:
                            pre = h_lp[:, :, :].rearrange("p t (b c w) -> p (t b) c w", c=2, w=w)
                            suf = h_ls[:, :, :].rearrange("p t (b c w) -> p (t b) c w", c=2, w=w)
                            nb = S // w
                            whole = lambda side: pre[:, :, side, w - 1:w].broadcast_to([P, nb, w])
                            tt(suf[:, :, 0, :], suf[:, :, 0, :], whole(1), ALU.add)
                            dve.drain()
                            tt(pre[:, :, 1, :], pre[:, :, 1, :], whole(0), ALU.add)
                            dve.drain().then_inc(h_scan_made, 1)
                    if lev:
                        take(lev - 1)
                take(9)
                c.add(h_exp_made, 9)
                c.add(h_scored, 40)
                meet()

            def mix1(l):
                meet()
                if l == 0:
                    tables()
                gates_first(l)
                for t in range(4):
                    conv(l, t)
                gates_second()
                meet()
                mlstm()
                hgrn(l)

                def on_outputs(j, b):
                    g = col("m_g", l, j) if j < 2 else col("h_g", l, j - 2)
                    stt(o[:, j, :], b[:, :], g, o[:, j, :], ALU.mult, ALU.mult).then_inc(n_applied, 1)
                    dve.drain()
                    gate = y[:, T_MO + j, :] if j < 2 else y[:, T_HG + j - 2, :]
                    tt(o[:, j, :], o[:, j, :], gate, ALU.mult)

                def on_heads(j, b):
                    g = col("q_g", l) if j < 4 else col("k_g", l)
                    t = y[:, T_SQ + j, :]
                    stt(t, b[:, :], g, t, ALU.mult, ALU.mult).then_inc(n_applied, 1)

                head_norm(4, 8, on_outputs)
                head_norm(6, 12, on_heads)
                rope(range(T_SQ, T_SK + 2))
                meet()
                attention(swa(l))
                meet()

            def lo_o(stack, l):
                h = operands(stack, l)[1]
                for k in range(DT):
                    lo_h(h, k, o[:, k, :])

            def add_to_x(k, final):
                def work(u, b):
                    tt(x[:, k, :], x[:, k, :], b[:, :], ALU.add).then_inc(bank_free, 1)
                    if final is not None:
                        dve.drain().then_inc(x_ready, 1)
                        lo_x(final[0], k, final[1])
                return work

            def out1(l):
                a = operands(1, l)[0]
                lo_o(1, l)
                for k in range(8):
                    step(add_to_x(k, (a, col("mlp_g", l, k))))

            def ffn1(l):
                a, h = operands(1, l)

                def chunk(last=False):
                    for j in range(8):
                        def hidden(u, b):
                            stt(y[:, 16 + j % 2, :], b[:, :], 0.0, r_x[:, :], ALU.max, ALU.mult).then_inc(bank_free, 1)
                            lo_h(h, j, y[:, 20 + j % 2, :])

                        step(hidden)
                    for k in range(8):
                        step(add_to_x(k, (a, col("ple_g", l, k)) if last else None))

                recip(r_x)
                chunk()
                with c.loop(FFN1_CHUNKS - 2, {h_hi_ready: 8}, 16):
                    chunk()
                chunk(last=True)

            def proj(l):
                h = operands(1, l)[1]
                for k in range(2):
                    lo_h(h, k, ple[:, k, :])
                for k in range(8):
                    step(lambda u, b: dve.tensor_copy(y[:, 8 + k, :], b[:, :]).then_inc(bank_free, 1))
                    if k == 0:
                        recip(r_x)

            def gate(l):
                h = operands(1, l)[1]

                def combine(k):
                    e = y[:, 8 + k, :]
                    stt(e, e, col("post_g", l, k), r_post[:, :], ALU.mult, ALU.mult)
                    dve.drain()
                    dve.wait_ge(act_made, c.since(act_made, k + 1))
                    tt(e, e, y[:, k, :], ALU.mult)
                    dve.drain()
                    tt(x[:, k, :], x[:, k, :], e, ALU.add)
                    dve.drain().then_inc(x_ready, 1)
                    lo_x(h, k, next_gain(l, k))

                for k in range(8):
                    step(lambda u, b: tt(y[:, k, :], b[:, :], r_x[:, :], ALU.mult).then_inc(bank_free, 1))
                    if k == 1:
                        recip(r_post)
                    if k >= 2:
                        combine(k - 2)
                combine(6)
                combine(7)
                c.add(act_made, 8)

            def post(name, l, gain):
                recip(r_post)
                for k in range(8):
                    stt(y[:, k, :], y[:, k, :], col(name, l, k), r_post[:, :], ALU.mult, ALU.mult)
                    dve.drain()
                    tt(x[:, k, :], x[:, k, :], y[:, k, :], ALU.add).then_inc(x_ready, 1)
                    if k and gain is not None:
                        lo_x(a_op, k - 1, col(gain[0], gain[1], k - 1))
                if gain is not None:
                    lo_x(a_op, 7, col(gain[0], gain[1], 7))

            def out2(l, name, gain):
                lo_o(2, l)
                for k in range(8):
                    step(lambda u, b: dve.tensor_copy(y[:, k, :], b[:, :]).then_inc(bank_free, 1))
                post(name, l, gain)

            def mix2(l):
                meet()
                if l == 0:
                    tables()
                    meet()
                rope(range(16))
                meet()
                attention(dilated() if l == 0 else differential())
                meet()
                if l == 1:
                    cut = 1.8446743e19
                    for j in range(8):
                        ts(n_sq[:, j, :], o[:, j, :], cut, -cut, ALU.min, ALU.max).then_inc(n_clamped, 1)
                    dve.wait_ge(n_root_made, c.count(n_root_made))
                    dve.reciprocal(n_row[0:8, 1, :], n_row[0:8, 0, :])
                    scale = 2.0 ** -32 * (1.0 - float(0.8 - 0.6 * np.exp(-0.3)))
                    ts(e_sq[0:8, 0, :], bank[5][0:8, :], 2.0 ** 64, scale, ALU.is_lt, ALU.mult)
                    dve.drain()
                    tt(n_row[0:8, 1, :], n_row[0:8, 1, :], e_sq[0:8, 0, :], ALU.mult)
                    dve.drain().then_inc(n_recip_made, 1)
                    for j in range(8):
                        dve.wait_ge(n_spread, c.count(n_spread))
                        stt(o[:, j, :], bank[6 + j % 2][:, :], col("sub_g"), o[:, j, :], ALU.mult, ALU.mult).then_inc(n_applied, 1)
                    meet()

            def kv(l):
                h = operands(2, l)[1]

                def scaled(u, b):
                    t = c.pick(u - first, 4)
                    tt(kv_y[:, t, :], b[:, 0:MEM], r_mem[:, :], ALU.mult).then_inc(bank_free, 1)

                for k in range(DT):
                    dve.wait_ge(h_hi_ready, c.count(h_hi_ready))
                    stt(h[1][:, k, 0:MEM], mem[:, k, :], col("mem_kv", l, k), f32(h[0][:, k, 0:MEM]),
                        ALU.mult, ALU.subtract).then_inc(h_ready, 1)
                first = c.unit
                for _ in range(4):
                    step(scaled)
                with c.loop(3, {}, 4):
                    for _ in range(4):
                        step(scaled)

            def xq(l):
                recip(r_x)
                for k in range(8):
                    step(lambda u, b: tt(y[:, k, :], b[:, :], r_x[:, :], ALU.mult).then_inc(bank_free, 1))

            def cross(l):
                meet()
                meet()
                attention(cross_attention())
                meet()

            def ffn2(l):
                h = operands(2, l)[1]
                recip(r_x)
                dve.wait_ge(y_zero, c.count(y_zero))

                def chunk(tiles):
                    for j in range(tiles):
                        def gate_(u, b):
                            tt(y[:, 16, :], b[:, :], r_x[:, :], ALU.mult).then_inc(bank_free, 1)

                        def up(u, b):
                            tt(y[:, 17, :], b[:, :], r_x[:, :], ALU.mult).then_inc(bank_free, 1)
                            dve.drain()
                            dve.wait_ge(act_made, c.count(act_made))
                            tt(y[:, 20 + j % 2, :], y[:, 17, :], y[:, 19, :], ALU.mult).then_inc(f_ready, 1)
                            lo_h(h, j, y[:, 20 + j % 2, :])

                        step(gate_)
                        step(up)
                    for k in range(8):
                        step(lambda u, b: tt(y[:, k, :], y[:, k, :], b[:, :], ALU.add).then_inc(bank_free, 1))

                with c.loop(2, {h_hi_ready: 8, act_made: 8}, 24):
                    chunk(8)
                chunk(6)
                post("ffn_post", l, ("mix_pre", l + 1) if l + 1 < LAYERS else None)

            load(0)
            for l in range(LAYERS):
                wide(1, l)
                mix1(l)
                out1(l)
                ffn1(l)
                proj(l)
                gate(l)
            for l in range(LAYERS):
                wide(2, l)
                mix2(l)
                out2(l, "mix_post", ("mem_pre", l))
                kv(l)
                xq(l)
                cross(l)
                out2(l, "mem_post", ("ffn_pre", l))
                ffn2(l)

        @block.gpsimd
        def _(pool):
            c = Counts(pool)

            def meet():
                pool.drain().then_inc(met["pool"], 1)
                pool.wait_ge(met["pe"], c.count(met["pe"]))
                pool.wait_ge(met["act"], c.count(met["act"]))
                pool.wait_ge(met["dve"], c.count(met["dve"]))

            def add_squares(cols=S):
                for k in range(8):
                    n = c.squares
                    pool.wait_ge(sq_ready, c.count(sq_ready))
                    s = sq[:, n % 2, 0:cols]
                    if k == 0:
                        if c.groups > 0:
                            pool.wait_ge(sum_ready, c.groups)
                        pool.tensor_copy(sq_sum[:, 0:cols], s).then_inc(sq_added, 1)
                    else:
                        pool.tensor_tensor(sq_sum[:, 0:cols], sq_sum[:, 0:cols], s, ALU.add).then_inc(sq_added, 1)
                    pool.drain()
                    c.squares += 1
                c.groups += 1

            def rope(tiles):
                for j, t in enumerate(tiles):
                    pool.wait_ge(rotated, c.count(rotated))
                    pool.tensor_tensor(y[:, t, :], y[:, t, :], cos_t[:, :], ALU.mult).then_inc(cos_taken, 1)

            def positions(name):
                pool.dma_start(pos_i[:, :], dram[name].partition_broadcast(P)).then_inc(pos_landed, 16)

            def load(l):
                add_squares(MEM)
                add_squares()

            def mix1(l):
                meet()
                if l == 0:
                    positions("positions")
                meet()
                meet()
                for n in range(16):
                    j = n % 4
                    pool.wait_ge(m_w_made, c.count(m_w_made))
                    w = m_w[:, n % 2, qs(j)]
                    pool.tensor_tensor(w, w, tri, ALU.mult).then_inc(m_w_masked, 1)
                meet()
                pool.memset(h_ls[:, :, :], 0.0)
                pool.memset(h_d[:, :, :, :], 0.0)
                meet()
                meet()
                meet()
                meet()
                rope(range(T_SQ, T_SK + 2))
                meet()
                meet()

            def out1(l):
                pool.dma_start(ple[:, :, :], dram["ple"][l].rearrange("p (a b) -> p a b", a=2)).then_inc(ple_landed, 16)
                add_squares()

            def mix2(l):
                meet()
                if l == 0:
                    positions("positions_2")
                    meet()
                    pool.dma_start(dil[:, :], dram["c_dilated"]).then_inc(dil_landed, 16)
                rope(range(16))
                if l == 0:
                    pool.wait_ge(dil_landed, c.count(dil_landed, 16))
                meet()
                meet()
                if l == 1:
                    meet()

            def out2(l):
                pool.dma_start(mem[:, :, :], dram["mem"].rearrange("p (a b) -> p a b", a=DT)).then_inc(mem_landed, 16)
                add_squares()
                add_squares()

            def cross(l):
                meet()
                meet()
                meet()

            def xo(l):
                add_squares()
                add_squares()
                if DT * (6 + 3 * l + 2) > 0:
                    pool.wait_ge(x_ready, DT * (6 + 3 * l + 2))
                pool.memset(y[:, 0:8, :], 0.0)
                pool.drain().then_inc(y_zero, 1)

            def ffn2(l):
                add_squares()
                if l + 1 < LAYERS:
                    add_squares()

            load(0)
            for l in range(LAYERS):
                mix1(l)
                out1(l)
                add_squares()
                add_squares()
                add_squares()
            for l in range(LAYERS):
                mix2(l)
                out2(l)
                cross(l)
                xo(l)
                ffn2(l)


def tiles(a):
    f, s = a.shape
    return a.reshape(f // P, P, s).transpose(1, 0, 2).reshape(P, -1)


def units(w, kt=KU):
    k, n = w.shape
    u = w.reshape(k // P, P, n // P, P).transpose(2, 1, 0, 3).reshape(n // P, P, k)
    if k < KU * P:
        u = np.concatenate([u, np.zeros((n // P, P, KU * P - k), w.dtype)], axis=2)
    return u


def pack_weights(i):
    out = []
    cols = np.array(win_columns())
    for l in range(LAYERS):
        w = np.where(cols[None, :] >= 0, i["w_in"][l][:, np.maximum(cols, 0)], np.float32(0))
        out += [units(w), units(i["w_out"][l])]
        for ch in range(FFN1_CHUNKS):
            part = slice(ch * 1024, ch * 1024 + 1024)
            out += [units(i["w_up"][l][:, part]), units(i["w_down"][l][part])]
        out += [units(i["w_ple_proj"][l]), units(i["w_ple_gate"][l])]
    for l in range(LAYERS):
        mixer = "ab"[l]
        out += [units(i[mixer + "_w_in_2"][0]), units(i[mixer + "_w_out_2"][0]), units(i["x_wkv_2"][l]),
                units(i["x_wq_2"][l]), units(i["x_wo_2"][l])]
        at = 0
        for n in FFN2_CHUNKS:
            part = slice(at * P, (at + n) * P)
            g, u = units(i["w_gate_up_2"][l][:, part]), units(i["w_gate_up_2"][l][:, FF2:][:, part])
            out += [np.stack([g, u], 1).reshape(-1, P, KU * P), units(i["w_down_2"][l][part])]
            at += n
    return np.concatenate(out)


def pack_vectors(i):
    cols = np.array(win_columns())
    vec = np.zeros((P, NV), np.float32)

    def put(name, layer, a):
        base, width = VCOL[name]
        vec[:, base + layer * width:base + (layer + 1) * width] = a

    for l in range(LAYERS):
        put("b_in", l, np.where(cols >= 0, i["b_in"][l][np.maximum(cols, 0)], np.float32(0)).reshape(-1, P).T)
        for name, src in (("in_g", "in_norm_g"), ("mlp_g", "mlp_norm_g"), ("ple_g", "ple_norm_g"), ("post_g", "ple_post_norm_g"),
                          ("conv_b", "mlstm_conv_b"), ("m_g", "mlstm_norm_g"), ("h_g", "hgrn_norm_g"),
                          ("lb_logit", "hgrn_lb_logits"), ("mix_pre", "mix_pre_g_2"), ("mix_post", "mix_post_g_2"),
                          ("mem_pre", "mem_pre_g_2"), ("mem_kv", "mem_kv_g_2"), ("mem_post", "mem_post_g_2"),
                          ("ffn_pre", "ffn_pre_g_2"), ("ffn_post", "ffn_post_g_2")):
            put(name, l, i[src][l].reshape(-1, P).T)
        put("conv_w", l, i["mlstm_conv_w"][l].reshape(16, P).T)
        put("q_g", l, np.tile(i["swa_q_norm_g"][l], 2)[:, None])
        put("k_g", l, np.tile(i["swa_k_norm_g"][l], 2)[:, None])
        put("sinks", l, np.tile(i["swa_sinks"][l], (P, 1)))
        vec[32:36, VCOL["f_b"][0] + l] = i["mlstm_f_bias"][l]
    put("sub_g", 0, i["b_sub_g_2"][0][:, None])
    base = VCOL["lam"][0]
    for j, name in enumerate(("q1", "q2", "k1", "k2")):
        vec[:64, base + j] = i[f"b_lam_{name}_2"][0]
    freq = np.zeros(64, np.float32)
    freq[0:8] = freq[8:16] = (500000.0 ** (-np.arange(0, 16, 2) / 16.0)).astype(np.float32)
    vec[:, VCOL["inv_freq"][0]] = np.tile(freq, 2)
    return vec


def kernel(**inputs):
    import concourse.bacc as bacc
    from concourse.bass_utils import run_bass_kernel_spmd as run

    i = {k: np.asarray(a) for k, a in inputs.items()}
    arrays = dict(constants(), weights=pack_weights(i), vec=pack_vectors(i), x=tiles(i["x"][0].T), mem=tiles(i["mem_2"][0].T),
                  ple=np.stack([tiles(i["p"][l, 0].T) for l in range(LAYERS)]),
                  positions=i["positions"][0], positions_2=i["positions_2"][0])
    arrays = {k: np.ascontiguousarray(a) for k, a in arrays.items()}
    nc = bacc.Bacc("TRN2", target_bir_lowering=False, num_devices=1)
    dram = {k: nc.dram_tensor(k, a.shape, mybir.dt.from_np(a.dtype), kind="ExternalInput").ap() for k, a in arrays.items()}
    out = nc.dram_tensor("out", (P, DT * S), F32, kind="ExternalOutput").ap()
    build(nc, dram, out)
    r = run(nc, [arrays], core_ids=[0])
    got = r.results[0]["out"]
    return got.reshape(P, DT, S).transpose(2, 1, 0).reshape(1, S, D)
```

```python
from contextlib import ExitStack

import numpy as np

import concourse.bass as bass
from concourse import mybir

F32 = mybir.dt.float32
F32R = mybir.dt.float32r
I32 = mybir.dt.int32
U8 = mybir.dt.uint8
ALU = mybir.AluOpType
ACT = mybir.ActivationFunctionType

P = 128
S = 512
ST = S // P
D = 1024
DT = D // P
MEM = 256
FF1 = 4096
FF2 = 2816
PLE = 256
LAYERS = 2
EPS = 1e-6
BIG = 1e30
KU = 8
SLOTS = 4

H4, H8 = 256, 512
_O = dict(mq=0, mk=256, mv=512, mo=768, mi=1024, mf=1028, hq=1032, hf=1288, hi=1544, hg=1800,
          sq=2056, sk=2568, sv=2696)


def win_columns():
    r = lambda a, n: list(range(a, a + n))
    cols = r(_O["mq"], 256) + r(_O["mk"], 256) + r(_O["mo"], 256) + r(_O["hq"], 256)
    cols += r(_O["hf"], 256) + r(_O["hg"], 256)
    cols += r(_O["mi"], 4) + [-1] * 28 + r(_O["mf"], 4) + [-1] * 92
    cols += r(_O["sq"], 512)
    cols += r(_O["sk"], 64) * 2 + r(_O["sk"] + 64, 64) * 2
    cols += r(_O["mv"], 256) + r(_O["hi"], 256) + r(_O["sv"], 128)
    return cols


T_MQ, T_MK, T_MO, T_HQ, T_HF, T_HG, T_GATE, T_SQ, T_SK, T_MV, T_HI, T_SV = 0, 2, 4, 6, 8, 10, 12, 13, 17, 19, 21, 23
WIN_EARLY = 16
WIN_T = 24

_VECS = [("in_g", 8, 2), ("b_in", 24, 2), ("mlp_g", 8, 2), ("ple_g", 8, 2), ("post_g", 8, 2),
         ("conv_w", 16, 2), ("conv_b", 4, 2), ("m_g", 2, 2), ("h_g", 2, 2), ("q_g", 1, 2), ("k_g", 1, 2),
         ("f_b", 1, 2), ("lb_logit", 2, 2), ("sinks", 8, 2),
         ("mix_pre", 8, 2), ("mix_post", 8, 2), ("mem_pre", 8, 2), ("mem_kv", 8, 2), ("mem_post", 8, 2),
         ("ffn_pre", 8, 2), ("ffn_post", 8, 2), ("sub_g", 1, 1), ("lam", 4, 1), ("inv_freq", 1, 1)]
VCOL, NV = {}, 0
for _n, _w, _l in _VECS:
    VCOL[_n] = (NV, _w)
    NV += _w * _l

FFN1_CHUNKS = 4
FFN2_CHUNKS = (8, 8, 6)
STREAM = []
for _l in range(LAYERS):
    STREAM += [(24 + 8 + 64, 8), (8, 2), (8, 8)]
for _l in range(LAYERS):
    STREAM += [(24 + 8 + 16 + 8 + 8 + 24 + 24 + 12, 8), (8, 6)]
UNITS = sum(n for n, _ in STREAM)
X_TILES = DT * 6 * LAYERS

_TWO_PI = 2 * np.pi
C1 = 6.28125
C2 = float(np.round((_TWO_PI - C1) * 2 ** 20) / 2 ** 20)
C3 = float(np.float32(_TWO_PI - C1 - C2))
MAGIC = 1.5 * 2.0 ** 23


def constants():
    i = np.arange(P)
    rot = np.zeros((P, P), np.float32)
    for base in (0, 64):
        for d in range(8):
            rot[base + d + 8, base + d] = -1.0
            rot[base + d, base + d + 8] = 1.0
    heads = np.zeros((20, 1280), np.float32)
    heads[np.arange(1280) // 64, np.arange(1280)] = 1.0
    halves = np.zeros((P, 38), np.float32)
    halves[:64, 18] = halves[64:, 19] = 1.0
    unit8 = np.zeros((P, 15), np.float32)
    unit8[:, 7] = 1.0
    q, k = np.arange(P)[:, None], np.arange(2 * P)[None, :]
    band = np.where((k > q) & (k <= q + P), 0.0, -BIG).astype(np.float32)
    delta = np.arange(P)[:, None] - (np.arange(896)[None, :] - 384)
    count = (abs(delta) <= 64) * 1 + ((delta % 4 == 0) & (abs(delta) <= 256)) + ((delta % 16 == 0) & (abs(delta) <= 1024))
    dilated = np.where(count > 0, 8.0 * np.log(np.maximum(count, 1)), -BIG).astype(np.float32)
    level = np.zeros((8, P, P), np.float32)
    for j in range(7):
        w = 2 ** j
        s_, l_ = i[:, None], i[None, :]
        level[j] = (s_ // (2 * w) == l_ // (2 * w)) & (s_ // w % 2 == 0) & (l_ // w % 2 == 1)
    level[7] = np.eye(P)
    tri = (i[:, None] <= i[None, :]).astype(np.float32)
    small = np.concatenate([np.eye(P, dtype=np.float32), rot, band, tri, halves, unit8], axis=1)
    return dict(c_small=small, c_heads=heads, c_dilated=dilated,
                c_level=np.ascontiguousarray(level.transpose(1, 0, 2)).reshape(P, 8 * P))


class Counts:

    def __init__(self, eng):
        self.eng, self.n, self.reg, self.per = eng, {}, None, {}
        self.unit = self.next = self.groups = self.squares = 0
        self.per_units = 0

    def count(self, sem, more=1):
        n = self.n[sem.name] = self.n.get(sem.name, 0) + more
        per = self.per.get(sem.name, 0) if self.reg is not None else 0
        return self.reg * per + n if per else n

    def by_unit(self, value, times=1):
        return self.reg * (self.per_units * times) + value if self.reg is not None else value

    def begun(self, value):
        return value > 0 or self.reg is not None

    def since(self, sem, value):
        return self.n.get(sem.name, 0) + value

    def add(self, sem, more):
        self.n[sem.name] = self.n.get(sem.name, 0) + more

    def loop(self, times, per, units):
        return _Loop(self, times, per, units)

    def pick(self, first, stride):
        return first if self.reg is None else self.reg * stride + first


class _Loop:
    def __init__(self, c, times, per, units):
        self.c, self.times, self.units = c, times, units
        self.per = {sem.name: n for sem, n in per.items()}
        self.fori = c.eng.Fori(0, times)

    def __enter__(self):
        c = self.c
        c.reg = self.fori.__enter__()
        c.per, c.per_units = self.per, self.units

    def __exit__(self, *a):
        self.fori.__exit__(*a)
        c = self.c
        c.reg = None
        for name, per in self.per.items():
            c.n[name] = c.n.get(name, 0) + (self.times - 1) * per
        c.unit += (self.times - 1) * self.units
        c.next += (self.times - 1) * self.units


def combined(k):
    return {0: [], 1: [], 2: [0], 3: [1, 2]}.get(k, [k - 1])


class Attention:

    def __init__(self, heads, comps, scale, key_tiles, scores, mask, sink, outputs):
        self.heads, self.comps, self.scale = heads, comps, scale
        self.key_tiles, self.scores, self.mask, self.sink, self.outputs = key_tiles, scores, mask, sink, outputs
        self.groups = [(h, q) for h in range(heads) for q in range(ST)]


def build(nc, dram, out):
    ctx = ExitStack()
    with ctx:
        sem = lambda name: ctx.enter_context(nc.semaphore(name))

        top = [(nc.sbuf_base + 63) // 64 * 64]

        def place(name, shape, dt=F32, at=None):
            size = int(np.prod(shape[1:])) * (1 if dt == U8 else 4)
            if at is None:
                at, top[0] = top[0], top[0] + (size + 63) // 64 * 64
            return nc.alloc_sbuf_tensor_at(name, shape, dt, offset=at)

        def region(size):
            at, top[0] = top[0], top[0] + size
            return at

        KB = 1024
        x = place("x", [P, DT, S])
        at_a, at_b = region(32 * KB), region(32 * KB)
        a_op = (place("a_hi", [P, DT, S], F32R, at_a), place("a_lo", [P, DT, S], F32R, at_a + 16 * KB))
        b_op = (place("b_hi", [P, DT, S], F32R, at_b), place("b_lo", [P, DT, S], F32R, at_b + 16 * KB))
        w_hi = place("w_hi", [P, SLOTS, KU * P], F32R)
        at_w = region(SLOTS * KU * P * 4)
        w_raw = place("w_raw", [P, SLOTS, KU * P], F32, at_w)
        w_lo = place("w_lo", [P, SLOTS, KU * P], F32R, at_w)
        y = place("y", [P, 24, S])
        at_o, at_v = region(16 * KB), region(16 * KB)
        o = place("o", [P, DT, S], F32, at_o)
        v = place("v", [P, ST, D], F32, at_v)
        sq = place("sq", [P, 2, S], F32, at_o)
        sq_sum = place("sq_sum", [P, S], F32, at_o + 4 * KB)
        root = place("root", [P, S], F32, at_o + 6 * KB)
        r_post = place("r_post", [P, S], F32, at_o + 8 * KB)
        mem = place("mem", [P, DT, MEM], F32, at_v)
        ple = place("ple", [P, 2, S], F32, at_v)
        small = place("small", [P, 4 * P + P + 38 + 15])
        ident, rot, band, tri = (small[:, a:b] for a, b in ((0, 128), (128, 256), (256, 512), (512, 640)))
        halves, unit8 = small[:, 640:678], small[:, 678:693]
        heads_c = place("heads_c", [4, 256])
        level = place("level", [P, 8, P], U8)
        vec = place("vec", [P, NV])
        der = place("der", [P, 64])
        r_x = place("r_x", [P, S])
        r_mem = place("r_mem", [P, MEM])
        cos_t, sin_t = place("cos_t", [P, S]), place("sin_t", [P, S])
        assert top[0] <= nc.sbuf_usable_end, (top[0], nc.sbuf_usable_end)
        eps, half_pi, ones = der[:, 0:1], der[:, 1:2], der[:, 2:3]
        lb, one_lb = der[:, 4:8], der[:, 8:12]
        neg_sink, lam, lam_e = der[:, 12:28], der[:, 28:29], der[:, 30:32]
        stat_n, stat_d, stat_s = der[:, 32:40], der[:, 40:48], der[:, 48:56]
        eps_big = der[:, 3:4]

        def in_a(name, shape, kb, dt=F32):
            return place(name, shape, dt, at_a + int(kb * KB))

        def in_b(name, shape, kb, dt=F32):
            return place(name, shape, dt, at_b + int(kb * KB))

        pos_i = in_b("pos_i", [P, S], 0, I32)
        ang = in_b("ang", [P, 3, S], 2)
        h_lp = in_a("h_lp", [P, 2, S], 0)
        h_ls = in_a("h_ls", [P, 2, S], 4)
        h_q = in_a("h_q", [P, 2, 2, S], 8)
        h_k = in_a("h_k", [P, 2, 2, S], 16)
        h_key = in_a("h_key", [P, 2, S], 24)
        h_neg = o[:, 4:6, :]
        h_d = in_b("h_d", [P, 4, ST, P], 0)
        h_o1 = in_b("h_o1", [P, 4, 2, P], 8)
        h_o2 = in_b("h_o2", [P, 4, 2, 2 * P], 12)
        m_rows = (in_b("m_row0", [P, 8, S], 0), in_a("m_row1", [P, 8, S], 8))
        m_end = in_b("m_end", [P, 2, S], 16)
        m_t = in_b("m_t", [P, 2, S], 20)
        m_w = in_b("m_w", [P, 2, S], 24)
        m_s = in_b("m_s", [P, 2, S], 28)
        m_col = in_a("m_col", [P, 16], 28)
        m_den = o[:, 6:8, :]
        n_sq = in_a("n_sq", [P, 10, S], 0)
        n_row = in_a("n_row", [20, 2, S], 20)
        e_sq = in_a("e_sq", [P, 2, S], 24)
        prob = in_b("prob", [P, 4, S], 0)
        prob_t = in_b("prob_t", [P, 2, ST, S], 8)
        dil = in_b("dil", [P, 896], 24)
        r_t = in_a("r_t", [P, 2, S], 28)

        bank = [ctx.enter_context(nc.psum_tensor(f"bank{i}", [P, S], F32)) for i in range(8)]
        S_BANK, T_BANK, O_BANK = (0, 1, 2, 5), (3, 4), (6, 7)
        SUM_BANK = 2
        G_BANK = (0, 1, 3, 4)

        loaded, vec_loaded, x_loaded, stored = sem("loaded"), sem("vec_loaded"), sem("x_loaded"), sem("stored")
        w_landed = [sem(f"w_landed{i}") for i in range(SLOTS)]
        w_hi_ready, w_lo_ready, unit_done, bank_free = sem("w_hi_ready"), sem("w_lo_ready"), sem("unit_done"), sem("bank_free")
        x_ready, a_hi_ready, a_ready = sem("x_ready"), sem("a_hi_ready"), sem("a_ready")
        h_hi_ready, h_ready = sem("h_hi_ready"), sem("h_ready")
        act_made, f_ready, y_zero = sem("act_made"), sem("f_ready"), sem("y_zero")
        sq_ready, sq_added, sum_ready, root_ready, recip_ready = (
            sem("sq_ready"), sem("sq_added"), sem("sum_ready"), sem("root_ready"), sem("recip_ready"))
        ple_landed, mem_first_landed, mem_landed, pos_landed, dil_landed, heads_landed = sem("ple_landed"), sem("mem_first_landed"), sem("mem_landed"), sem("pos_landed"), sem("dil_landed"), sem("heads_landed")
        met = {n: sem(f"met_{n}") for n in ("pe", "act", "dve", "pool")}
        m_ended, e_gated, y_scaled, h_key_made, h_zeroed, y_made, conv_made, gates_split, gates_log, gates_made, cols_made = (
            sem("m_ended"), sem("e_gated"), sem("y_scaled"), sem("h_key_made"), sem("h_zeroed"), sem("y_made"), sem("conv_made"), sem("gates_split"), sem("gates_log"), sem("gates_made"), sem("cols_made"))
        m_scored, m_gap_made, m_w_made, m_w_masked, m_s_made, m_summed, m_den_made = (
            sem("m_scored"), sem("m_gap_made"), sem("m_w_made"), sem("m_w_masked"), sem("m_s_made"),
            sem("m_summed"), sem("m_den_made"))
        h_f_made, h_exp_made, h_ops_made, h_scan_made, h_scored, h_taken, h_summed = (
            sem("h_f_made"), sem("h_exp_made"), sem("h_ops_made"), sem("h_scan_made"), sem("h_scored"),
            sem("h_taken"), sem("h_summed"))
        n_clamped, n_squared, n_summed, n_root_made, n_recip_made, n_spread, n_applied = (
            sem("n_clamped"), sem("n_squared"), sem("n_summed"), sem("n_root_made"), sem("n_recip_made"),
            sem("n_spread"), sem("n_applied"))
        angles_made, rotated, sin_taken, cos_taken = sem("angles_made"), sem("rotated"), sem("sin_taken"), sem("cos_taken")
        lam_made, lam_summed, lam_exp = sem("lam_made"), sem("lam_summed"), sem("lam_exp")
        scores_ready, max_ready, exp_ready, norm_ready = sem("scores_ready"), sem("max_ready"), sem("exp_ready"), sem("norm_ready")
        transposed, probs_t_ready, out_ready, out_taken = sem("transposed"), sem("probs_t_ready"), sem("out_ready"), sem("out_taken")

        def col(name, layer=0, k=0):
            base, width = VCOL[name]
            return vec[:, base + layer * width + k:base + layer * width + k + 1]

        def operands(stack, layer):
            return (b_op, a_op) if stack == 1 and layer == 1 else (a_op, b_op)

        def f32(ap):
            return ap.bitcast(F32)

        def half(t, p, cols):
            return t[64 * p:64 * p + 64, cols]

        def qs(q):
            return slice(q * P, (q + 1) * P)

        def swa(layer):
            def scores(h, q, c):
                ks = slice(max(q - 1, 0) * P, (q + 1) * P)
                r = slice(64 * (h % 2), 64 * (h % 2) + 64)
                return [(y[r, T_SQ + h // 2, qs(q)], y[r, T_SK + h // 4, ks])]

            def outputs(h):
                r = slice(64 * (h % 2), 64 * (h % 2) + 64)
                vc = slice(512 + 64 * (h // 4), 576 + 64 * (h // 4))
                mm = [(qs(q), v[:, kt, vc], prob_t[:, h % 2, i, qs(q)], i == 0, i == len(kts(q)) - 1)
                      for q in range(ST) for i, kt in enumerate(kts(q))]
                return [(r, mm, o[r, 4 + h // 2, :])]

            kts = lambda q: [q - 1, q] if q else [0]
            return Attention(8, 1, 0.125, kts, scores, lambda q: band if q else band[:, P:], lambda h: (layer, h), outputs)

        def all_keys(n):
            return lambda q: list(range(n))

        def pv(h, vc, n):
            return [(slice(0, S), v[:, kt, vc], prob_t[:, h % 2, kt, :], kt == 0, kt == n - 1) for kt in range(n)]

        def dilated():
            def scores(h, q, c):
                r = slice(64 * (h % 2), 64 * (h % 2) + 64)
                return [(y[r, h // 2, qs(q)], y[r, 8 + h // 2, :])]

            def outputs(h):
                r = slice(64 * (h % 2), 64 * (h % 2) + 64)
                return [(r, pv(h, slice(64 * h, 64 * h + 64), ST), o[r, h // 2, :])]

            return Attention(16, 1, 0.125, all_keys(ST), scores, lambda q: dil[:, 384 - P * q:896 - P * q], None, outputs)

        def differential():
            def scores(h, q, c):
                r = slice(64 * c, 64 * c + 64)
                return [(y[r, h, qs(q)], y[r, 8 + h, :])]

            return Attention(8, 2, 0.125, all_keys(ST), scores, None, None,
                             lambda h: [(slice(0, P), pv(h, slice(P * h, P * h + P), ST), o[:, h, :])])

        kv_y = y[:, 8:16, :].rearrange("p t (a s) -> p (t a) s", a=2)

        def cross_attention():
            def scores(h, q, c):
                return [(y[:, 2 * h + i, qs(q)], kv_y[:, 2 * h + i, :]) for i in range(2)]

            return Attention(4, 1, 0.0625, all_keys(2), scores, None, None,
                             lambda h: [(slice(0, P), pv(h, slice(P * t, P * t + P), 2), o[:, t, :])
                                        for t in (2 * h, 2 * h + 1)])

        block = ctx.enter_context(nc.Block())

        @block.sync
        def _(sp):
            c = Counts(sp)
            sp.dma_start(vec[:, :], dram["vec"]).then_inc(vec_loaded, 16)
            sp.dma_start(x[:, :, :], dram["x"].rearrange("p (a b) -> p a b", a=DT)).then_inc(x_loaded, 16)

            def load_rest():
                sp.dma_start(small[:, :], dram["c_small"]).then_inc(loaded, 16)
                sp.dma_start(heads_c[:, :], dram["c_heads"][0:4, 0:256]).then_inc(loaded, 16)
                sp.dma_start(o[:, 6:8, :], dram["c_level"].rearrange("p (a b) -> p a b", a=2)).then_inc(loaded, 16)
                sp.dma_start(mem[:, :, :], dram["mem"].rearrange("p (a b) -> p a b", a=DT)).then_inc(mem_first_landed, 16)

            def load_unit(j, width):
                u = c.unit
                if c.begun(u - SLOTS + 1):
                    sp.wait_ge(unit_done, c.by_unit(u - SLOTS + 1))
                src = dram["weights"][c.pick(u, SLOTS), :, 0:width]
                sp.dma_start(w_raw[:, u % SLOTS, 0:width], src).then_inc(w_landed[u % SLOTS], 16)
                c.unit += 1

            runs = []
            for n, kt in STREAM:
                if runs and runs[-1][1] == kt:
                    runs[-1][0] += n
                else:
                    runs.append([n, kt])
            for n, kt in runs:
                turns = n // SLOTS
                if c.unit == 0:
                    for j in range(SLOTS):
                        load_unit(j, kt * P)
                    load_rest()
                    turns -= 1
                if turns:
                    with c.loop(turns, {}, SLOTS):
                        for j in range(SLOTS):
                            load_unit(j, kt * P)
            for k in range(DT):
                sp.wait_ge(x_ready, X_TILES - DT + k + 1)
                sp.dma_start(out[:, k * S:(k + 1) * S], x[:, k, :]).then_inc(stored, 16)
            sp.wait_ge(stored, 16 * DT)

        @block.tensor
        def _(pe):
            c = Counts(pe)
            mm = pe.matmul
            att = dict(n=0, t=0, o=0)

            def meet():
                pe.drain().then_inc(met["pe"], 1)
                pe.wait_ge(met["act"], c.count(met["act"]))
                pe.wait_ge(met["dve"], c.count(met["dve"]))
                pe.wait_ge(met["pool"], c.count(met["pool"]))

            def unit(op, kt=8, cols=S, ready=None):
                u = c.unit
                pe.wait_ge(w_lo_ready, c.by_unit(u + 1))
                if c.begun(u - 3):
                    pe.wait_ge(bank_free, c.by_unit(u - 3))
                for k in range(kt):
                    if ready is not None:
                        pe.wait_ge(ready, c.count(ready))
                    last = products(u, k, op, kt, cols)
                last.then_inc(unit_done, 1)
                c.unit += 1

            def products(u, k, op, kt, cols):
                ks = slice(k * P, (k + 1) * P)
                hi, lo = op
                for n, (w, t) in enumerate(((w_hi, hi), (w_hi, lo), (w_lo, hi))):
                    last = mm(bank[G_BANK[u % 4]][:, 0:cols], w[:, u % SLOTS, ks], t[:, k, 0:cols],
                              start=(k == 0 and n == 0), stop=(k == kt - 1 and n == 2))
                return last

            def pair(op, ready, cols=S):
                u = c.unit
                pe.wait_ge(w_lo_ready, u + 2)
                if u - 2 > 0:
                    pe.wait_ge(bank_free, u - 2)
                for k in range(8):
                    pe.wait_ge(ready, c.count(ready))
                    products(u, k, op, 8, cols) if k < 7 else products(u, k, op, 8, cols).then_inc(unit_done, 1)
                    last = products(u + 1, k, op, 8, cols)
                last.then_inc(unit_done, 1)
                c.unit += 2

            def sum_squares(cols=S):
                pe.wait_ge(sq_added, c.count(sq_added, 8))
                if c.groups > 0:
                    pe.wait_ge(root_ready, c.groups)
                c.groups += 1
                mm(bank[SUM_BANK][:, 0:cols], ones.broadcast_to([P, P]), sq_sum[:, 0:cols],
                   start=True, stop=True).then_inc(sum_ready, 1)

            def values(tiles):
                for t in tiles:
                    if att["t"] - 1 > 0:
                        pe.wait_ge(probs_t_ready, att["t"] - 1)
                    for tb in range(t.shape[-1] // P):
                        last = pe.transpose(bank[T_BANK[att["t"] % 2]][:, qs(tb)], t[:, qs(tb)], ident)
                    last.then_inc(transposed, 1)
                    att["t"] += 1

            def attention(a):
                def scores(g):
                    h, q = a.groups[g]
                    for comp in range(a.comps):
                        n = att["n"]
                        if n - 3 > 0:
                            pe.wait_ge(exp_ready, n - 3)
                        ops = a.scores(h, q, comp)
                        for i, (l, r) in enumerate(ops):
                            last = mm(bank[S_BANK[n % 4]][:, 0:r.shape[-1]], l, r,
                                      start=(i == 0), stop=(i == len(ops) - 1))
                        last.then_inc(scores_ready, 1)
                        att["n"] += 1

                def outputs(h, tiles):
                    if tiles > 0:
                        pe.wait_ge(probs_t_ready, tiles)
                    for rows, mms, _ in a.outputs(h):
                        if att["o"] - 1 > 0:
                            pe.wait_ge(out_taken, att["o"] - 1)
                        for cols, l, r, start, stop in mms:
                            last = mm(bank[O_BANK[att["o"] % 2]][rows, cols], l, r, start=start, stop=stop)
                        last.then_inc(out_ready, 1)
                        att["o"] += 1

                n0, t0 = att["n"], att["t"]
                ahead = 4 // a.comps - 1
                for g in range(ahead):
                    scores(g)
                for g, (h, q) in enumerate(a.groups):
                    if g + ahead < len(a.groups):
                        scores(g + ahead)
                    pe.wait_ge(norm_ready, c.count(norm_ready))
                    if att["t"] - 1 > 0:
                        pe.wait_ge(probs_t_ready, att["t"] - 1)
                    pr = prob[:, (n0 + g * a.comps) % 4, :]
                    for i in range(len(a.key_tiles(q))):
                        last = pe.transpose(bank[T_BANK[att["t"] % 2]][:, qs(i)], pr[:, qs(i)], ident)
                    last.then_inc(transposed, 1)
                    att["t"] += 1
                    if q == 0 and h > 0:
                        outputs(h - 1, t0 + g)
                outputs(a.heads - 1, att["t"])

            def head_norm(tiles, rows, window, spread):
                pe.wait_ge(n_squared, c.since(n_squared, tiles))
                for j in range(tiles):
                    last = mm(bank[5][0:rows, :], window(j), n_sq[:, j, :], start=(j == 0), stop=(j == tiles - 1))
                last.then_inc(n_summed, 1)
                pe.wait_ge(n_recip_made, c.since(n_recip_made, 1))
                for j in range(tiles):
                    if j - 1 > 0:
                        pe.wait_ge(n_applied, c.since(n_applied, j - 1))
                    mm(bank[6 + j % 2][:, :], spread(j), n_row[0:rows, 1, :], start=True, stop=True).then_inc(n_spread, 1)
                c.add(n_squared, tiles)
                c.add(n_recip_made, 1)
                c.add(n_applied, tiles)
                meet()

            def head_norm64(tiles):
                pe.wait_ge(heads_landed, c.count(heads_landed, 32))
                head_norm(tiles, 2 * tiles, lambda j: halves[:, 18 - 2 * j:18 - 2 * j + 2 * tiles],
                          lambda j: y[0:2 * tiles, j // ST, qs(j % ST)])

            def rope(tiles):
                for j, t in enumerate(tiles):
                    if j - 1 > 0:
                        pe.wait_ge(sin_taken, c.since(sin_taken, j - 1))
                    mm(bank[j % 2][:, :], rot, y[:, t, :], start=True, stop=True).then_inc(rotated, 1)
                c.add(sin_taken, len(tiles))

            def memory():
                sum_squares(MEM)
                pe.wait_ge(lam_made, c.count(lam_made))
                mm(bank[5][:, 0:2], ones.broadcast_to([P, P]), lam_e, start=True, stop=True).then_inc(lam_summed, 1)

            def wide(stack, l):
                op = operands(stack, l)[0]
                pair(op, a_ready)
                sum_squares()
                for _ in range(2):
                    unit(op)
                first = stack == 1 and l == 0
                if first:
                    for _ in range(WIN_EARLY - 8):
                        unit(op)
                    memory()
                with c.loop(WIN_T // 4 - (3 if first else 1), {}, 4):
                    for _ in range(4):
                        unit(op)

            def mlstm(l):
                m_row = m_rows[l]
                for tb in range(ST):
                    mm(bank[5][:, 4 * tb:4 * tb + 4], m_row[0:4, 3, qs(tb)], ident[0:4, 0:4], start=True, stop=True)
                for p in range(2):
                    last = mm(bank[6 + p][:, :], heads_c[0:4, qs(p)], m_row[0:4, 5, :], start=True, stop=True)
                last.then_inc(cols_made, 1)
                meet()
                blocks = [(h, j) for h in range(4) for j in range(ST)]

                def scores(n):
                    h, j = blocks[n]
                    r = slice(64 * (h % 2), 64 * (h % 2) + 64)
                    if j == 0:
                        if 4 * (h - 1) > 0:
                            pe.wait_ge(m_gap_made, c.since(m_gap_made, 4 * (h - 1)))
                        mm(bank[2 + h % 2][:, :], heads_c[0:4, 64 * h:64 * h + 1].broadcast_to([4, P]),
                           m_row[0:4, 4, :], start=True, stop=True)
                    if n - 1 > 0:
                        pe.wait_ge(m_s_made, c.since(m_s_made, n - 1))
                    mm(bank[n % 2][:, j * P:], y[r, T_MK + h // 2, qs(j)], y[r, T_MQ + h // 2, j * P:],
                       start=True, stop=True).then_inc(m_scored, 1)

                scores(0)
                for n, (h, j) in enumerate(blocks):
                    if n + 1 < len(blocks):
                        scores(n + 1)
                    pe.wait_ge(m_s_made, c.since(m_s_made, n + 1))
                    r = slice(64 * (h % 2), 64 * (h % 2) + 64)
                    w = m_s[:, n % 2, j * P:]
                    num, den = bank[6 - 2 * (h // 2)], bank[7 - 2 * (h // 2)]
                    mm(num[r, j * P:], v[:, j, 64 * h:64 * h + 64], w, start=(j == 0), stop=(j == 3))
                    mm(den[r, j * P:], ones.broadcast_to([P, 64]), w, start=(j == 0), stop=(j == 3)).then_inc(m_summed, 1)
                c.add(m_gap_made, 16)
                c.add(m_s_made, 16)
                meet()

            def hgrn():
                for lev in range(10):
                    if lev < 9:
                        pe.wait_ge(h_ops_made, c.since(h_ops_made, lev + 1))
                        pe.wait_ge(h_key_made, c.since(h_key_made, lev + 1))
                    for h in range(4):
                        n = 4 * lev + h
                        r = slice(64 * (h % 2), 64 * (h % 2) + 64)
                        if lev < 9:
                            q_, k_ = h_q[r, lev % 2, h // 2, :], h_k[r, lev % 2, h // 2, :]
                        else:
                            q_, k_ = y[r, T_HQ + h // 2, :], h_key[r, h // 2, :]
                        if n - 3 > 0:
                            pe.wait_ge(h_taken, c.since(h_taken, n - 3))
                        if lev == 7:
                            pairs = [(qs(0), qs(0), qs(1)), (qs(1), qs(2), qs(3))]
                        elif lev == 8:
                            late = slice(2 * P, 4 * P)
                            pairs = [(slice(0, 2 * P), qs(0), late), (late, qs(1), late)]
                        else:
                            pairs = [(qs(i), qs(i), qs(i)) for i in range(ST)]
                        for cols, ks, ls in pairs:
                            last = mm(bank[n % 4][:, cols], k_[:, ks], q_[:, ls], start=True, stop=True)
                        last.then_inc(h_scored, 1)
                c.add(h_ops_made, 9)
                c.add(h_key_made, 9)
                pe.wait_ge(h_taken, c.since(h_taken, 40))
                c.add(h_taken, 40)
                pe.wait_ge(m_ended, c.count(m_ended, 2))
                late = slice(2 * P, 4 * P)
                for h in range(4):
                    r = slice(64 * (h % 2), 64 * (h % 2) + 64)
                    vc = slice(256 + 64 * h, 320 + 64 * h)
                    terms = [(qs(i), i, h_d[:, h, i, :]) for i in range(ST)]
                    terms += [(qs(1), 0, h_o1[:, h, 0, :]), (qs(3), 2, h_o1[:, h, 1, :]),
                              (late, 0, h_o2[:, h, 0, :]), (late, 1, h_o2[:, h, 1, :])]
                    for i, (cols, kt, rhs) in enumerate(terms):
                        last = mm(bank[6 + h // 2][r, cols], v[:, kt, vc], rhs, start=(i == 0),
                                  stop=(i == len(terms) - 1), skip_group_check=True)
                last.then_inc(h_summed, 1)
                meet()

            def mix1(l):
                meet()
                values([y[:, t, :] for t in range(T_MV, T_SV + 1)])
                meet()
                mlstm(l)
                hgrn()
                head_norm64(10)
                rope(range(T_SQ, T_SK + 2))
                meet()
                attention(swa(l))
                meet()

            def out_product(stack, l):
                h = operands(stack, l)[1]
                pair(h, h_ready)
                for _ in range(6):
                    unit(h)

            def ffn1(l):
                a, h = operands(1, l)

                def chunk(first=False):
                    if first:
                        pair(a, a_ready)
                        sum_squares()
                    for j in range(2 if first else 0, 8):
                        unit(a)
                    for j in range(8):
                        unit(h, ready=h_ready if j == 0 else None)

                chunk(True)
                with c.loop(FFN1_CHUNKS - 2, {h_ready: 8}, 16):
                    chunk()
                chunk()

            def proj(l):
                h = operands(1, l)[1]
                pe.wait_ge(h_ready, c.count(h_ready, 2))
                for j in range(8):
                    unit(h, kt=2)
                    if j == 0:
                        sum_squares()

            def gate(l):
                a = operands(1, l)[0]
                pair(a, a_ready)
                sum_squares()
                for _ in range(6):
                    unit(a)

            def mix2(l):
                meet()
                rope(range(16))
                values([y[:, 16 + t, :] for t in range(8)])
                meet()
                attention(dilated() if l == 0 else differential())
                meet()
                if l == 1:
                    head_norm(8, 8, lambda j: unit8[:, 7 - j:15 - j], lambda j: ident[0:8, j:j + 1].broadcast_to([8, P]))

            def kv(l):
                h = operands(2, l)[1]
                pair(h, h_ready, cols=MEM)
                for _ in range(2):
                    unit(h, cols=MEM)
                with c.loop(3, {}, 4):
                    for _ in range(4):
                        unit(h, cols=MEM)

            def xq(l):
                a = operands(2, l)[0]
                pair(a, a_ready)
                sum_squares()
                for _ in range(6):
                    unit(a)

            def cross(l):
                meet()
                values([kv_y[:, 8 + t, :] for t in range(8)])
                meet()
                attention(cross_attention())
                meet()

            def ffn2(l):
                a, h = operands(2, l)

                def chunk(tiles, first=False):
                    if first:
                        pair(a, a_ready)
                        sum_squares()
                    for _ in range(2 if first else 0, 2 * tiles):
                        unit(a)
                    pe.wait_ge(h_ready, c.count(h_ready, tiles))
                    for _ in range(8):
                        unit(h, kt=tiles)

                chunk(8, first=True)
                chunk(8)
                chunk(6)
                sum_squares()

            def out2(l):
                out_product(2, l)
                sum_squares()

            for l in range(LAYERS):
                wide(1, l)
                mix1(l)
                out_product(1, l)
                ffn1(l)
                proj(l)
                gate(l)
            for l in range(LAYERS):
                wide(2, l)
                mix2(l)
                out2(l)
                kv(l)
                xq(l)
                cross(l)
                out2(l)
                ffn2(l)

        @block.scalar
        def _(act):
            c = Counts(act)
            f = act.activation
            att = dict(n=0, t=0, o=0, group=[], outs=[])

            def meet():
                act.drain().then_inc(met["act"], 1)
                act.wait_ge(met["pe"], c.count(met["pe"]))
                act.wait_ge(met["dve"], c.count(met["dve"]))
                act.wait_ge(met["pool"], c.count(met["pool"]))

            widths = [kt * P for n, kt in STREAM for _ in range(n)]

            def split_hi():
                u = c.next
                if u == UNITS:
                    return
                act.wait_ge(w_landed[u % SLOTS], c.by_unit(16 * (u // SLOTS + 1), 4))
                if c.begun(u - SLOTS + 1):
                    act.wait_ge(unit_done, c.by_unit(u - SLOTS + 1))
                f(w_hi[:, u % SLOTS, 0:widths[u]], w_raw[:, u % SLOTS, 0:widths[u]], ACT.Copy).then_inc(w_hi_ready, 1)
                c.next += 1

            def step(work=None):
                if work is not None:
                    work(c.unit)
                if c.next < c.unit + SLOTS:
                    split_hi()
                c.unit += 1

            def split_and_root():
                split_hi()
                root_of_mean()
                split_hi()

            def load_sqrt():
                f(der[:, 56:57], eps, ACT.Sqrt)

            def taken(u):
                act.wait_ge(bank_free, c.by_unit(u + 1))

            def square(src, cols=S):
                n = c.squares
                if n - 1 > 0:
                    act.wait_ge(sq_added, n - 1)
                f(sq[:, n % 2, 0:cols], src, ACT.Square).then_inc(sq_ready, 1)
                c.squares += 1

            def root_of_mean(cols=S):
                act.wait_ge(sum_ready, c.count(sum_ready))
                if c.groups > 0:
                    act.wait_ge(recip_ready, c.groups)
                c.groups += 1
                f(root[:, 0:cols], bank[SUM_BANK][:, 0:cols], ACT.Sqrt, bias=eps, scale=1.0 / D).then_inc(root_ready, 1)

            def round_x(dst, k, gain, wait=True):
                if wait:
                    act.wait_ge(x_ready, c.count(x_ready))
                f(dst[0][:, k, :], x[:, k, :], ACT.Copy, scale=gain).then_inc(a_hi_ready, 1)
                square(x[:, k, :])

            def values(n, tok=ST):
                for i in range(n):
                    act.wait_ge(transposed, c.count(transposed))
                    f(v[:, 0:tok, qs(i)], bank[T_BANK[att["t"] % 2]][:, 0:tok * P].rearrange("p (a b) -> p a b", a=tok),
                      ACT.Copy).then_inc(probs_t_ready, 1)
                    att["t"] += 1

            def attention(a):
                def exps(g):
                    h, q = a.groups[g]
                    nk = P * len(a.key_tiles(q))
                    for comp in range(a.comps):
                        n = att["n"]
                        s = n % 8
                        act.wait_ge(max_ready, c.count(max_ready))
                        if n >= 4:
                            if att["group"][n - 4] + 1 > 0:
                                act.wait_ge(transposed, att["group"][n - 4] + 1)
                        last = f(prob[:, n % 4, 0:nk], bank[S_BANK[n % 4]][:, 0:nk], ACT.Exp, bias=stat_n[:, s:s + 1],
                                 scale=a.scale, accum_out=stat_d[:, s:s + 1])
                        if a.sink is not None:
                            last = f(stat_s[:, s:s + 1], col("sinks", *a.sink(h)), ACT.Exp, bias=stat_n[:, s:s + 1])
                        last.then_inc(exp_ready, 1)
                        att["group"].append(att["t0"] + g)
                        att["n"] += 1

                att["t0"] = att["t"]
                exps(0)
                for g, (h, q) in enumerate(a.groups):
                    if g + 1 < len(a.groups):
                        exps(g + 1)
                    act.wait_ge(transposed, c.count(transposed))
                    if q == 0 and len(att["outs"]) >= 2:
                        if att["outs"][-2] > 0:
                            act.wait_ge(out_ready, att["outs"][-2])
                    nk = len(a.key_tiles(q))
                    f(prob_t[:, h % 2, 0:nk, qs(q)],
                      bank[T_BANK[att["t"] % 2]][:, 0:nk * P].rearrange("p (a b) -> p a b", a=nk),
                      ACT.Copy).then_inc(probs_t_ready, 1)
                    att["t"] += 1
                    if q == ST - 1:
                        att["o"] += len(a.outputs(h))
                        att["outs"].append(att["o"])

            def head_norm(tiles, rows, src, scale=1.0, width=64, bias=None, clamped=False):
                for j in range(tiles):
                    if clamped:
                        act.wait_ge(n_clamped, c.since(n_clamped, j + 1))
                    f(n_sq[:, j, :], src(j), ACT.Square, scale=scale).then_inc(n_squared, 1)
                c.add(n_clamped, tiles if clamped else 0)
                act.wait_ge(n_summed, c.count(n_summed))
                f(n_row[0:rows, 0, :], bank[5][0:rows, :], ACT.Sqrt, bias=(eps if bias is None else bias)[0:rows, :],
                  scale=1.0 / width).then_inc(n_root_made, 1)
                meet()

            def load(l):
                act.wait_ge(vec_loaded, 16)
                act.wait_ge(lam_made, c.count(lam_made))
                act.wait_ge(x_loaded, 16)
                for k in range(DT):
                    round_x(a_op, k, col("in_g", 0, k), wait=False)
                    if k < SLOTS - 1:
                        split_hi()

            def memory():
                root_of_mean(MEM)
                act.wait_ge(lam_summed, c.count(lam_summed))
                f(lam_e, bank[5][:, 0:2], ACT.Exp).then_inc(lam_exp, 1)
                f(lb[:, 2:4], lb[:, 0:2], ACT.Sigmoid)
                f(one_lb[:, 2:4], lb[:, 0:2], ACT.Sigmoid, scale=-1.0)
                act.drain()
                f(lb[:, 0:2], lb[:, 0:2], ACT.Copy, scale=0.0).then_inc(lam_exp, 1)

            def wide(stack, l):
                m_row = m_rows[l]

                def bias(u):
                    taken(u)
                    t = c.pick(u - first, 4)
                    b = VCOL["b_in"][0] + l * WIN_T
                    f(y[:, t, :], y[:, t, :], ACT.Identity, bias=vec[:, bass.ds(t + b, 1)])

                first = c.unit
                work = bias if stack == 1 else None
                split_and_root()
                for _ in range(4):
                    step(work)
                if l == 0:
                    tables()
                if stack == 1:
                    act.drain().then_inc(y_made, 1)
                    for _ in range(2):
                        step(work)
                    for t in range(4):
                        act.wait_ge(conv_made, c.count(conv_made))
                        f(y[:, T_MQ + t, :], o[:, t, :], ACT.Silu)
                        if t < 2:
                            step(work)
                turns = WIN_EARLY // 4 - 2 if stack == 1 else WIN_T // 4 - 1
                if stack == 1 and l == 0:
                    act.drain()
                    act.wait_ge(mem_first_landed, 16)
                    for k in range(DT):
                        square(mem[:, k, :], MEM)
                        if k % 2:
                            step(work)
                    memory()
                    turns -= 1
                with c.loop(turns, {}, 4):
                    for _ in range(4):
                        step(work)
                if stack == 2:
                    return
                act.drain().then_inc(y_made, 1)
                act.wait_ge(gates_split, c.count(gates_split))
                f(m_row[0:4, 2, :], m_row[0:4, 2, :], ACT.Exp)
                act.drain()
                f(m_row[0:4, 2, :], m_row[0:4, 2, :], ACT.Ln, bias=ones[0:4, :]).then_inc(gates_log, 1)
                step(work)
                f(y[:, T_MO:T_MO + 2, :], y[:, T_MO:T_MO + 2, :], ACT.Sigmoid)
                f(h_neg, y[:, T_HF:T_HF + 2, :], ACT.Sigmoid, scale=-1.0)
                f(y[:, T_HF:T_HF + 2, :], y[:, T_HF:T_HF + 2, :], ACT.Sigmoid)
                step(work)
                f(y[:, T_HQ:T_HQ + 2, :], y[:, T_HQ:T_HQ + 2, :], ACT.Silu)
                f(y[:, T_HG:T_HG + 2, :], y[:, T_HG:T_HG + 2, :], ACT.Silu)
                for _ in range(3):
                    step(work)
                act.wait_ge(gates_made, c.count(gates_made))
                f(m_row[0:4, 5, :], m_row[0:4, 5, :], ACT.Exp)
                for _ in range(3):
                    step(work)

            def tables():
                act.wait_ge(angles_made, c.count(angles_made))
                f(sin_t[:, :], ang[:, 0, :], ACT.Sin)
                f(cos_t[:, :], ang[:, 2, :], ACT.Sin, bias=half_pi, scale=-1.0)

            def mlstm():
                act.wait_ge(cols_made, c.count(cols_made))
                f(m_col[:, :], bank[5][:, 0:16], ACT.Copy)
                for p in range(2):
                    f(m_end[:, p, :], bank[6 + p][:, :], ACT.Copy)
                meet()
                for n in range(16):
                    j = n % 4
                    act.wait_ge(m_gap_made, c.since(m_gap_made, n + 1))
                    if n - 1 > 0:
                        act.wait_ge(m_s_made, c.since(m_s_made, n - 1))
                    f(m_w[:, n % 2, j * P:], m_t[:, n % 2, j * P:], ACT.Exp, scale=-1.0).then_inc(m_w_made, 1)
                c.add(m_gap_made, 16)
                c.add(m_s_made, 16)
                act.wait_ge(m_summed, c.count(m_summed, 16))
                for p in range(2):
                    f(m_den[:, p, :], bank[7 - 2 * p][:, :], ACT.Abs).then_inc(m_den_made, 1)
                meet()

            def hgrn():
                for lev in range(9):
                    if 4 * (lev - 1) > 0:
                        act.wait_ge(h_scored, c.since(h_scored, 4 * (lev - 1)))
                    if lev > 0:
                        act.wait_ge(h_scan_made, c.since(h_scan_made, lev))
                    f(h_q[:, lev % 2, :, :], h_lp[:, :, :], ACT.Exp)
                    f(h_k[:, lev % 2, :, :], h_ls[:, :, :], ACT.Exp).then_inc(h_exp_made, 1)
                c.add(h_scored, 40)
                c.add(h_scan_made, 8)
                act.wait_ge(h_summed, c.count(h_summed))
                for p in range(2):
                    f(o[:, 2 + p, :], bank[6 + p][:, :], ACT.Copy)
                meet()

            def mix1(l):
                meet()
                values(5)
                act.wait_ge(h_f_made, c.count(h_f_made))
                f(h_lp[:, :, :], y[:, T_HF:T_HF + 2, :], ACT.Ln)
                meet()
                mlstm()
                hgrn()
                head_norm(10, 20, lambda j: o[:, j, :] if j < 4 else y[:, T_SQ + j - 4, :])
                meet()
                attention(swa(l))
                meet()

            def round_o(stack, l):
                h = operands(stack, l)[1]
                for k in range(DT):
                    f(h[0][:, k, :], o[:, k, :], ACT.Copy).then_inc(h_hi_ready, 1)
                load_sqrt()

            def out1(l):
                a = operands(1, l)[0]
                round_o(1, l)
                for k in range(8):
                    step(lambda u: round_x(a, k, col("mlp_g", l, k)))

            def ffn1(l):
                a, h = operands(1, l)

                def chunk(first=False, last=False):
                    for j in range(8):
                        def hidden(u):
                            taken(u)
                            f(y[:, 20 + j % 2, :], y[:, 16 + j % 2, :], ACT.Square)
                            f(h[0][:, j, :], y[:, 16 + j % 2, :], ACT.Square).then_inc(h_hi_ready, 1)

                        if first and j == 0:
                            split_and_root()
                        step(hidden)
                    for k in range(8):
                        step((lambda u: round_x(a, k, col("ple_g", l, k))) if last else None)

                chunk(first=True)
                with c.loop(FFN1_CHUNKS - 2, {}, 16):
                    chunk()
                chunk(last=True)

            def proj(l):
                h = operands(1, l)[1]
                act.wait_ge(ple_landed, c.count(ple_landed, 16))
                for k in range(2):
                    f(h[0][:, k, :], ple[:, k, :], ACT.Copy).then_inc(h_hi_ready, 1)
                for k in range(8):
                    def squares(u):
                        taken(u)
                        square(y[:, 8 + k, :])

                    if k == 0:
                        split_hi()
                        root_of_mean()
                    step(squares)

            def gate(l):
                h = operands(1, l)[1]
                split_hi()
                split_hi()
                for k in range(8):
                    def sigmoid(u):
                        taken(u)
                        f(y[:, k, :], y[:, k, :], ACT.Sigmoid).then_inc(act_made, 1)

                    step(sigmoid)
                    if k == 1:
                        root_of_mean()
                    for j in combined(k):
                        round_x(h, j, next_gain(l, j))
                load_sqrt()
                round_x(h, 7, next_gain(l, 7))

            def next_gain(l, k):
                return col("in_g", l + 1, k) if l + 1 < LAYERS else col("mix_pre", 0, k)

            def out2(l):
                round_o(2, l)
                for k in range(8):
                    def squares(u):
                        taken(u)
                        square(y[:, k, :])

                    step(squares)

            def post(name):
                root_of_mean()
                for k in range(8):
                    if name is not None:
                        round_x(a_op, k, col(name[0], name[1], k))

            def mix2(l):
                meet()
                values(8)
                meet()
                attention(dilated() if l == 0 else differential())
                meet()
                if l == 1:
                    head_norm(8, 8, lambda j: n_sq[:, j, :], 2.0 ** -32, P, eps_big, clamped=True)

            def kv(l):
                h = operands(2, l)[1]
                act.wait_ge(mem_landed, c.count(mem_landed, 16))
                for k in range(DT):
                    f(h[0][:, k, 0:MEM], mem[:, k, :], ACT.Copy, scale=col("mem_kv", l, k)).then_inc(h_hi_ready, 1)
                root_of_mean()
                for k in range(8):
                    step()
                    round_x(a_op, k, col("mem_pre", l, k))
                with c.loop(2, {}, 4):
                    for _ in range(4):
                        step()

            def xq(l):
                split_and_root()
                for _ in range(8):
                    step()

            def cross(l):
                meet()
                values(8, 2)
                meet()
                attention(cross_attention())
                meet()

            def ffn2(l):
                h = operands(2, l)[1]
                split_and_root()

                def chunk(tiles, last=False):
                    for j in range(tiles):
                        def silu(u):
                            taken(u)
                            f(y[:, 19, :], y[:, 16, :], ACT.Silu).then_inc(act_made, 1)

                        def hidden(u):
                            act.wait_ge(f_ready, c.count(f_ready))
                            f(h[0][:, j, :], y[:, 20 + j % 2, :], ACT.Copy).then_inc(h_hi_ready, 1)

                        step(silu)
                        step(hidden)
                    if last:
                        load_sqrt()
                    for k in range(8):
                        def squares(u):
                            taken(u)
                            square(y[:, k, :])

                        step(squares if last else None)

                chunk(8)
                chunk(8)
                chunk(6, last=True)
                post(("mix_pre", l + 1) if l + 1 < LAYERS else None)

            load(0)
            for l in range(LAYERS):
                wide(1, l)
                mix1(l)
                out1(l)
                ffn1(l)
                proj(l)
                gate(l)
            for l in range(LAYERS):
                wide(2, l)
                mix2(l)
                out2(l)
                kv(l)
                xq(l)
                cross(l)
                out2(l)
                post(("ffn_pre", l))
                ffn2(l)

        @block.vector
        def _(dve):
            c = Counts(dve)
            tt, ts, stt = dve.tensor_tensor, dve.tensor_scalar, dve.scalar_tensor_tensor
            att = dict(n=0, o=0)
            widths = [kt * P for n, kt in STREAM for _ in range(n)]

            def meet():
                dve.drain().then_inc(met["dve"], 1)
                dve.wait_ge(met["pe"], c.count(met["pe"]))
                dve.wait_ge(met["act"], c.count(met["act"]))
                dve.wait_ge(met["pool"], c.count(met["pool"]))

            def split_lo():
                u = c.next
                if u == UNITS:
                    return
                dve.wait_ge(w_hi_ready, c.by_unit(u + 1))
                w = slice(0, widths[u])
                tt(w_lo[:, u % SLOTS, w], w_raw[:, u % SLOTS, w], f32(w_hi[:, u % SLOTS, w]), ALU.subtract).then_inc(w_lo_ready, 1)
                c.next += 1

            def step(work):
                u = c.unit
                dve.wait_ge(unit_done, c.by_unit(u + 1))
                work(u, bank[G_BANK[u % 4]])
                if c.next < u + SLOTS:
                    split_lo()
                c.unit += 1

            def split_and_recip(dst):
                split_lo()
                recip(dst)
                split_lo()

            def recip(dst, cols=S):
                dve.wait_ge(root_ready, c.count(root_ready))
                dve.reciprocal(dst[:, 0:cols], root[:, 0:cols]).then_inc(recip_ready, 1)
                dve.drain()

            def lo_x(dst, k, gain):
                dve.wait_ge(a_hi_ready, c.count(a_hi_ready))
                stt(dst[1][:, k, :], x[:, k, :], gain, f32(dst[0][:, k, :]), ALU.mult, ALU.subtract).then_inc(a_ready, 1)

            def lo_h(h, k, src):
                dve.wait_ge(h_hi_ready, c.count(h_hi_ready))
                tt(h[1][:, k, :], src, f32(h[0][:, k, :]), ALU.subtract).then_inc(h_ready, 1)

            def next_gain(l, k):
                return col("in_g", l + 1, k) if l + 1 < LAYERS else col("mix_pre", 0, k)

            def attention(a):
                def maxima(g):
                    h, q = a.groups[g]
                    nk = P * len(a.key_tiles(q))
                    for _ in range(a.comps):
                        n = att["n"]
                        b, s = bank[S_BANK[n % 4]][:, 0:nk], stat_n[:, n % 8:n % 8 + 1]
                        dve.wait_ge(scores_ready, c.count(scores_ready))
                        if a.mask is not None:
                            dve.tensor_tensor_reduce(out=b, in0=b, in1=a.mask(q), scale=1.0, scalar=-3e38,
                                                     op0=ALU.add, op1=ALU.max, accum_out=s)
                        else:
                            dve.reduce_max(s, b, mybir.AxisListType.X)
                        dve.drain()
                        if a.sink is not None:
                            l, hh = a.sink(h)
                            ts(s, s, -a.scale, neg_sink[:, 8 * l + hh:8 * l + hh + 1], ALU.mult, ALU.min).then_inc(max_ready, 1)
                        else:
                            ts(s, s, -a.scale, None, ALU.mult).then_inc(max_ready, 1)
                        att["n"] += 1

                def normalise(g):
                    h, q = a.groups[g]
                    nk = P * len(a.key_tiles(q))
                    dve.wait_ge(exp_ready, c.count(exp_ready, a.comps))
                    ns = [n0 + g * a.comps + i for i in range(a.comps)]
                    for n in ns:
                        d = stat_d[:, n % 8:n % 8 + 1]
                        if a.sink is not None:
                            tt(d, d, stat_s[:, n % 8:n % 8 + 1], ALU.add)
                            dve.drain()
                        dve.reciprocal(d, d)
                    dve.drain()
                    p0, d0 = prob[:, ns[0] % 4, 0:nk], stat_d[:, ns[0] % 8:ns[0] % 8 + 1]
                    if a.comps == 1:
                        ts(p0, p0, d0, None, ALU.mult).then_inc(norm_ready, 1)
                    else:
                        p1, d1 = prob[:, ns[1] % 4, 0:nk], stat_d[:, ns[1] % 8:ns[1] % 8 + 1]
                        ts(p1, p1, d1, lam, ALU.mult, ALU.mult)
                        dve.drain()
                        stt(p0, p0, d0, p1, ALU.mult, ALU.subtract).then_inc(norm_ready, 1)

                def take(h):
                    for rows, _, dst in a.outputs(h):
                        dve.wait_ge(out_ready, c.count(out_ready))
                        dve.tensor_copy(dst, bank[O_BANK[att["o"] % 2]][rows, :]).then_inc(out_taken, 1)
                        att["o"] += 1

                n0 = att["n"]
                ahead = 2 // a.comps
                for g in range(ahead):
                    maxima(g)
                for g, (h, q) in enumerate(a.groups):
                    normalise(g)
                    if g + ahead < len(a.groups):
                        maxima(g + ahead)
                    if q == 1 and h > 0:
                        take(h - 1)
                take(a.heads - 1)

            def head_norm(tiles, rows, apply):
                dve.wait_ge(n_root_made, c.count(n_root_made))
                dve.reciprocal(n_row[0:rows, 1, :], n_row[0:rows, 0, :])
                dve.drain().then_inc(n_recip_made, 1)
                for j in range(tiles):
                    dve.wait_ge(n_spread, c.count(n_spread))
                    apply(j, bank[6 + j % 2])
                meet()

            def rope(tiles):
                for j, t in enumerate(tiles):
                    dve.wait_ge(rotated, c.since(rotated, j + 1))
                    tt(r_t[:, j % 2, :], bank[j % 2][:, :], sin_t[:, :], ALU.mult).then_inc(sin_taken, 1)
                    dve.drain()
                    dve.wait_ge(cos_taken, c.since(cos_taken, j + 1))
                    tt(y[:, t, :], y[:, t, :], r_t[:, j % 2, :], ALU.add)
                c.add(rotated, len(tiles))
                c.add(cos_taken, len(tiles))

            def load(l):
                dve.memset(eps, EPS)
                dve.memset(eps_big, EPS * 2.0 ** -64)
                dve.memset(half_pi, float(np.pi / 2))
                dve.memset(ones, 1.0)
                dve.memset(one_lb[:, 0:2], 1.0)
                dve.wait_ge(vec_loaded, 16)
                b = VCOL["lb_logit"][0]
                tt(lb[:, 0:2], vec[:, b + 2:b + 4], vec[:, b:b + 2], ALU.subtract)
                b = VCOL["sinks"][0]
                ts(neg_sink, vec[:, b:b + 16], -1.0, None, ALU.mult)
                b = VCOL["lam"][0]
                tt(lam_e, vec[:, b:b + 2], vec[:, b + 2:b + 4], ALU.mult)
                dve.drain().then_inc(lam_made, 1)
                dve.wait_ge(x_loaded, 16)
                for k in range(DT):
                    lo_x(a_op, k, col("in_g", 0, k))
                    if k < SLOTS - 1:
                        split_lo()

            def memory():
                recip(r_mem, MEM)
                dve.wait_ge(lam_exp, c.count(lam_exp, 2))
                ts(lam, lam_e[:, 0:1], lam_e[:, 1:2], float(0.8 - 0.6 * np.exp(-0.3)), ALU.subtract, ALU.add)
                dve.wait_ge(loaded, 48)
                dve.tensor_copy(level[:, :, :].rearrange("p a b -> p (a b)"), o[:, 6:8, :].rearrange("p a b -> p (a b)"))

            def wide(stack, l):
                def scaled(u, b):
                    t = c.pick(u - first, 4)
                    tt(y[:, t, :], b[:, :], r_x[:, :], ALU.mult).then_inc(bank_free, 1)

                first = c.unit
                split_and_recip(r_x)
                for _ in range(4):
                    step(scaled)
                if l == 0:
                    tables()
                if stack == 1:
                    dve.wait_ge(y_made, c.count(y_made))
                    for t in range(4):
                        conv(l, t)
                        step(scaled)
                turns = WIN_EARLY // 4 - 2 if stack == 1 else WIN_T // 4 - 1
                if stack == 1 and l == 0:
                    for _ in range(4):
                        step(scaled)
                    memory()
                    turns -= 1
                with c.loop(turns, {}, 4):
                    for _ in range(4):
                        step(scaled)
                if stack == 2:
                    return
                dve.wait_ge(y_made, c.count(y_made))
                gates_first(l)
                for _ in range(2):
                    step(scaled)
                gates_second(l)
                for _ in range(6):
                    step(scaled)

            def tables():
                dve.wait_ge(pos_landed, c.count(pos_landed, 16))
                r, t, n = ang[:, 0, :], ang[:, 1, :], ang[:, 2, :]
                dve.tensor_copy(t, pos_i[:, :])
                dve.drain()
                ts(r, t, col("inv_freq"), None, ALU.mult)
                dve.drain()
                ts(t, r, float(1 / _TWO_PI), MAGIC, ALU.mult, ALU.add)
                dve.drain()
                ts(t, t, MAGIC, None, ALU.subtract)
                dve.drain()
                for part in (C1, C2, C3):
                    stt(r, t, -part, r, ALU.mult, ALU.add)
                    dve.drain()
                ts(r, r, 3.1415925, -3.1415925, ALU.min, ALU.max)
                dve.drain()
                stt(n, r, -1.0, r, ALU.mult, ALU.max)
                dve.drain().then_inc(angles_made, 1)

            def gates_first(l):
                m_row = m_rows[l]
                g = y[32:36, T_GATE, :]
                b = VCOL["f_b"][0] + l
                ts(m_row[0:4, 0, :], g, vec[32:36, b:b + 1], None, ALU.add)
                dve.drain()
                ts(m_row[0:4, 1, :], m_row[0:4, 0, :], 0.0, None, ALU.min)
                stt(m_row[0:4, 2, :], m_row[0:4, 0, :], -1.0, m_row[0:4, 0, :], ALU.mult, ALU.min)
                dve.memset(m_row[0:4, 7, :], 0.0)
                dve.drain().then_inc(gates_split, 1)

            def gates_second(l):
                row = lambda i: m_rows[l][0:4, i, :]
                dve.wait_ge(gates_log, c.count(gates_log))
                tt(row(0), row(1), row(2), ALU.subtract)
                dve.drain()
                dve.tensor_tensor_scan(row(6), row(0), row(7), 0.0, ALU.add, ALU.add)
                dve.drain()
                tt(row(3), y[0:4, T_GATE, :], row(6), ALU.subtract)
                dve.drain()
                dve.tensor_tensor_scan(row(4), row(3), row(3), 0.0, ALU.max, ALU.max)
                dve.drain()
                tt(row(5), row(6), row(4), ALU.add)
                dve.drain()
                ts(row(5), row(5), -1.0, 88.0, ALU.mult, ALU.min)
                dve.drain().then_inc(gates_made, 1)

            def conv(l, t):
                w = lambda j: col("conv_w", l, 4 * j + t)
                u, acc = y[:, T_MQ + t, :], o[:, t, :]
                ts(acc, u, w(3), col("conv_b", l, t), ALU.mult, ALU.add)
                for back in (1, 2, 3):
                    dve.drain()
                    last = stt(acc[:, back:], u[:, :S - back], w(3 - back), acc[:, back:], ALU.mult, ALU.add)
                last.then_inc(conv_made, 1)

            def mlstm():
                meet()

                def gap(n):
                    h, j = n // 4, n % 4
                    dve.wait_ge(m_scored, c.since(m_scored, n + 1))
                    if n - 1 > 0:
                        dve.wait_ge(m_w_made, c.since(m_w_made, n - 1))
                    ts(m_t[:, n % 2, j * P:], bank[2 + h % 2][:, j * P:], m_col[:, 4 * j + h:4 * j + h + 1], 0.0,
                       ALU.subtract, ALU.max).then_inc(m_gap_made, 1)

                gap(0)
                for n in range(16):
                    j = n % 4
                    if n + 1 < 16:
                        gap(n + 1)
                    dve.wait_ge(m_w_masked, c.since(m_w_masked, n + 1))
                    if n - 1 > 0:
                        dve.wait_ge(m_summed, c.since(m_summed, n - 1))
                    stt(m_s[:, n % 2, j * P:], bank[n % 2][:, j * P:], 0.125, m_w[:, n % 2, j * P:],
                        ALU.mult, ALU.mult).then_inc(m_s_made, 1)
                c.add(m_scored, 16)
                c.add(m_w_made, 16)
                c.add(m_w_masked, 16)
                c.add(m_summed, 16)
                meet()

            def mlstm_end(p):
                dve.wait_ge(m_den_made, c.count(m_den_made))
                tt(m_den[:, p, :], m_den[:, p, :], m_end[:, p, :], ALU.max)
                dve.drain()
                dve.reciprocal(m_den[:, p, :], m_den[:, p, :])
                dve.drain()
                tt(o[:, p, :], bank[6 - 2 * p][:, :], m_den[:, p, :], ALU.mult).then_inc(m_ended, 1)

            def decay(l):
                for t in range(2):
                    k = 2 * l + t
                    ts(h_key[:, t, :], h_neg[:, t, :], one_lb[:, k:k + 1], None, ALU.mult)
                    ts(y[:, T_HF + t, :], y[:, T_HF + t, :], one_lb[:, k:k + 1], lb[:, k:k + 1], ALU.mult, ALU.add)
                dve.drain()
                last = ts(y[:, T_HF:T_HF + 2, :], y[:, T_HF:T_HF + 2, :], 2.0 ** -63, None, ALU.max)
                last.then_inc(h_f_made, 1)

            def hgrn():
                dve.wait_ge(h_zeroed, c.count(h_zeroed))

                def take(lev):
                    for h in range(4):
                        n = 4 * lev + h
                        dve.wait_ge(h_scored, c.since(h_scored, n + 1))
                        b = bank[n % 4]
                        if lev == 7:
                            last = dve.tensor_copy(h_o1[:, h, :, :], b[:, 0:2 * P].rearrange("p (a b) -> p a b", a=2))
                        elif lev == 8:
                            last = dve.tensor_copy(h_o2[:, h, :, :], b[:, :].rearrange("p (a b) -> p a b", a=2))
                        else:
                            m = level[:, min(lev, 7), :].unsqueeze(1).broadcast_to([P, ST, P])
                            last = dve.copy_predicated(h_d[:, h, :, :], m, b[:, :].rearrange("p (a b) -> p a b", a=ST))
                        last.then_inc(h_taken, 1)

                for lev in range(10):
                    if lev < 9:
                        w = 2 ** lev
                        b = lev % 2
                        dve.wait_ge(h_exp_made, c.since(h_exp_made, lev + 1))
                        tt(h_q[:, b, :, :], h_q[:, b, :, :], y[:, T_HQ:T_HQ + 2, :], ALU.mult).then_inc(h_ops_made, 1)
                        if lev < 8:
                            pre = h_lp[:, :, :].rearrange("p t (b c w) -> p (t b) c w", c=2, w=w)
                            suf = h_ls[:, :, :].rearrange("p t (b c w) -> p (t b) c w", c=2, w=w)
                            nb = S // w
                            whole = lambda side: pre[:, :, side, w - 1:w].broadcast_to([P, nb, w])
                            tt(suf[:, :, 0, :], suf[:, :, 0, :], whole(1), ALU.add)
                            dve.drain()
                            tt(pre[:, :, 1, :], pre[:, :, 1, :], whole(0), ALU.add)
                            dve.drain().then_inc(h_scan_made, 1)
                    if lev < 2:
                        mlstm_end(lev)
                    if lev:
                        take(lev - 1)
                take(9)
                c.add(h_exp_made, 9)
                c.add(h_scored, 40)
                meet()

            def mix1(l):
                meet()
                decay(l)
                meet()
                mlstm()
                hgrn()

                def on_outputs(j, b):
                    g = col("m_g", l, j) if j < 2 else col("h_g", l, j - 2)
                    stt(o[:, j, :], b[:, :], g, o[:, j, :], ALU.mult, ALU.mult).then_inc(n_applied, 1)
                    dve.drain()
                    gate = y[:, T_MO + j, :] if j < 2 else y[:, T_HG + j - 2, :]
                    tt(o[:, j, :], o[:, j, :], gate, ALU.mult)

                def on_tiles(j, b):
                    if j < 4:
                        on_outputs(j, b)
                        return
                    j -= 4
                    g = col("q_g", l) if j < 4 else col("k_g", l)
                    t = y[:, T_SQ + j, :]
                    stt(t, b[:, :], g, t, ALU.mult, ALU.mult).then_inc(n_applied, 1)

                head_norm(10, 20, on_tiles)
                rope(range(T_SQ, T_SK + 2))
                meet()
                attention(swa(l))
                meet()

            def lo_o(stack, l):
                h = operands(stack, l)[1]
                for k in range(DT):
                    lo_h(h, k, o[:, k, :])

            def add_to_x(k, final):
                def work(u, b):
                    tt(x[:, k, :], x[:, k, :], b[:, :], ALU.add).then_inc(bank_free, 1)
                    if final is not None:
                        dve.drain().then_inc(x_ready, 1)
                        lo_x(final[0], k, final[1])
                return work

            def out1(l):
                a = operands(1, l)[0]
                lo_o(1, l)
                for k in range(8):
                    step(add_to_x(k, (a, col("mlp_g", l, k))))

            def ffn1(l):
                a, h = operands(1, l)

                def chunk(last=False):
                    for j in range(8):
                        def hidden(u, b):
                            stt(y[:, 16 + j % 2, :], b[:, :], 0.0, r_x[:, :], ALU.max, ALU.mult).then_inc(bank_free, 1)
                            lo_h(h, j, y[:, 20 + j % 2, :])

                        step(hidden)
                    for k in range(8):
                        step(add_to_x(k, (a, col("ple_g", l, k)) if last else None))

                split_and_recip(r_x)
                chunk()
                with c.loop(FFN1_CHUNKS - 2, {h_hi_ready: 8}, 16):
                    chunk()
                chunk(last=True)

            def proj(l):
                h = operands(1, l)[1]
                for k in range(2):
                    lo_h(h, k, ple[:, k, :])
                split_lo()
                for k in range(8):
                    step(lambda u, b: dve.tensor_copy(y[:, 8 + k, :], b[:, :]).then_inc(bank_free, 1))
                    if k == 0:
                        recip(r_x)

            def gate(l):
                h = operands(1, l)[1]

                def combine(k):
                    e = y[:, 8 + k, :]
                    stt(e, e, col("post_g", l, k), r_post[:, :], ALU.mult, ALU.mult)
                    dve.drain()
                    dve.wait_ge(act_made, c.since(act_made, k + 1))
                    tt(e, e, y[:, k, :], ALU.mult).then_inc(e_gated, 1)

                split_lo()
                split_lo()
                for k in range(8):
                    step(lambda u, b: tt(y[:, k, :], b[:, :], r_x[:, :], ALU.mult).then_inc(bank_free, 1))
                    if k == 1:
                        recip(r_post)
                    for j in combined(k):
                        combine(j)
                        if j:
                            lo_x(h, j - 1, next_gain(l, j - 1))
                combine(7)
                lo_x(h, 6, next_gain(l, 6))
                lo_x(h, 7, next_gain(l, 7))
                c.add(act_made, 8)

            def post_tile(name, l, k):
                stt(y[:, k, :], y[:, k, :], col(name, l, k), r_post[:, :], ALU.mult, ALU.mult)
                dve.drain()
                tt(x[:, k, :], x[:, k, :], y[:, k, :], ALU.add).then_inc(x_ready, 1)

            def post(name, l, gain):
                recip(r_post)
                for k in range(8):
                    post_tile(name, l, k)
                    if k and gain is not None:
                        lo_x(a_op, k - 1, col(gain[0], gain[1], k - 1))
                if gain is not None:
                    lo_x(a_op, 7, col(gain[0], gain[1], 7))

            def out2(l):
                lo_o(2, l)
                for k in range(8):
                    step(lambda u, b: dve.tensor_copy(y[:, k, :], b[:, :]).then_inc(bank_free, 1))

            def mix2(l):
                meet()
                rope(range(16))
                meet()
                attention(dilated() if l == 0 else differential())
                meet()
                if l == 1:
                    cut = 1.8446743e19
                    for j in range(8):
                        ts(n_sq[:, j, :], o[:, j, :], cut, -cut, ALU.min, ALU.max).then_inc(n_clamped, 1)
                    dve.wait_ge(n_root_made, c.count(n_root_made))
                    dve.reciprocal(n_row[0:8, 1, :], n_row[0:8, 0, :])
                    scale = 2.0 ** -32 * (1.0 - float(0.8 - 0.6 * np.exp(-0.3)))
                    ts(e_sq[0:8, 0, :], bank[5][0:8, :], 2.0 ** 64, scale, ALU.is_lt, ALU.mult)
                    dve.drain()
                    tt(n_row[0:8, 1, :], n_row[0:8, 1, :], e_sq[0:8, 0, :], ALU.mult)
                    dve.drain().then_inc(n_recip_made, 1)
                    for j in range(8):
                        dve.wait_ge(n_spread, c.count(n_spread))
                        stt(o[:, j, :], bank[6 + j % 2][:, :], col("sub_g"), o[:, j, :], ALU.mult, ALU.mult).then_inc(n_applied, 1)
                    meet()

            def kv(l):
                h = operands(2, l)[1]

                def scaled(u, b):
                    t = c.pick(u - first, 4)
                    tt(kv_y[:, t, :], b[:, 0:MEM], r_mem[:, :], ALU.mult).then_inc(bank_free, 1)

                for k in range(DT):
                    dve.wait_ge(h_hi_ready, c.count(h_hi_ready))
                    stt(h[1][:, k, 0:MEM], mem[:, k, :], col("mem_kv", l, k), f32(h[0][:, k, 0:MEM]),
                        ALU.mult, ALU.subtract).then_inc(h_ready, 1)
                first = c.unit
                recip(r_post)
                for k in range(8):
                    step(scaled)
                    stt(y[:, k, :], y[:, k, :], col("mix_post", l, k), r_post[:, :], ALU.mult, ALU.mult).then_inc(y_scaled, 1)
                    if k:
                        lo_x(a_op, k - 1, col("mem_pre", l, k - 1))
                lo_x(a_op, 7, col("mem_pre", l, 7))
                with c.loop(2, {}, 4):
                    for _ in range(4):
                        step(scaled)

            def xq(l):
                split_and_recip(r_x)
                for k in range(8):
                    step(lambda u, b: tt(y[:, k, :], b[:, :], r_x[:, :], ALU.mult).then_inc(bank_free, 1))

            def cross(l):
                meet()
                meet()
                attention(cross_attention())
                meet()

            def ffn2(l):
                h = operands(2, l)[1]
                split_and_recip(r_x)
                dve.wait_ge(y_zero, c.count(y_zero))

                def chunk(tiles):
                    for j in range(tiles):
                        def gate_(u, b):
                            tt(y[:, 16, :], b[:, :], r_x[:, :], ALU.mult).then_inc(bank_free, 1)

                        def up(u, b):
                            tt(y[:, 17, :], b[:, :], r_x[:, :], ALU.mult).then_inc(bank_free, 1)
                            dve.drain()
                            dve.wait_ge(act_made, c.count(act_made))
                            tt(y[:, 20 + j % 2, :], y[:, 17, :], y[:, 19, :], ALU.mult).then_inc(f_ready, 1)
                            lo_h(h, j, y[:, 20 + j % 2, :])

                        step(gate_)
                        step(up)
                    for k in range(8):
                        step(lambda u, b: tt(y[:, k, :], y[:, k, :], b[:, :], ALU.add).then_inc(bank_free, 1))

                chunk(8)
                chunk(8)
                chunk(6)
                post("ffn_post", l, ("mix_pre", l + 1) if l + 1 < LAYERS else None)

            load(0)
            for l in range(LAYERS):
                wide(1, l)
                mix1(l)
                out1(l)
                ffn1(l)
                proj(l)
                gate(l)
            for l in range(LAYERS):
                wide(2, l)
                mix2(l)
                out2(l)
                kv(l)
                xq(l)
                cross(l)
                out2(l)
                post("mem_post", l, ("ffn_pre", l))
                ffn2(l)

        @block.gpsimd
        def _(pool):
            c = Counts(pool)

            def meet():
                pool.drain().then_inc(met["pool"], 1)
                pool.wait_ge(met["pe"], c.count(met["pe"]))
                pool.wait_ge(met["act"], c.count(met["act"]))
                pool.wait_ge(met["dve"], c.count(met["dve"]))

            def add_squares(cols=S, before=None):
                for k in range(8):
                    if before is not None:
                        before(k)
                    n = c.squares
                    pool.wait_ge(sq_ready, c.count(sq_ready))
                    s = sq[:, n % 2, 0:cols]
                    if k == 0:
                        if c.groups > 0:
                            pool.wait_ge(sum_ready, c.groups)
                        pool.tensor_copy(sq_sum[:, 0:cols], s).then_inc(sq_added, 1)
                    else:
                        pool.tensor_tensor(sq_sum[:, 0:cols], sq_sum[:, 0:cols], s, ALU.add).then_inc(sq_added, 1)
                    pool.drain()
                    c.squares += 1
                c.groups += 1

            def ahead(k, made, tile):
                for j in ([0, 1] if k == 0 else [k + 1]):
                    if j < 8:
                        pool.wait_ge(made, c.count(made))
                        pool.tensor_tensor(x[:, j, :], x[:, j, :], y[:, tile + j, :], ALU.add).then_inc(x_ready, 1)

            def rope(tiles):
                for j, t in enumerate(tiles):
                    pool.wait_ge(rotated, c.count(rotated))
                    pool.tensor_tensor(y[:, t, :], y[:, t, :], cos_t[:, :], ALU.mult).then_inc(cos_taken, 1)

            def positions(name):
                pool.dma_start(pos_i[:, :], dram[name].partition_broadcast(P)).then_inc(pos_landed, 16)

            def load(l):
                positions("positions")
                add_squares()
                add_squares(MEM)

            def mix1(l):
                meet()
                pool.memset(h_ls[:, :, :], 0.0)
                meet()
                meet()
                for n in range(16):
                    j = n % 4
                    pool.wait_ge(m_w_made, c.count(m_w_made))
                    w = m_w[:, n % 2, qs(j)]
                    pool.tensor_tensor(w, w, tri, ALU.mult).then_inc(m_w_masked, 1)
                meet()
                pool.memset(h_d[:, :, :, :], 0.0).then_inc(h_zeroed, 1)
                for lev in range(9):
                    pool.wait_ge(h_exp_made, c.count(h_exp_made))
                    k = h_k[:, lev % 2, :, :]
                    pool.tensor_tensor(k, k, h_key[:, :, :], ALU.mult).then_inc(h_key_made, 1)
                    if lev == 0:
                        pool.dma_start(y[0:20, 0:2, :], dram["c_heads"][:, 0:1024].rearrange("p (a b) -> p a b", a=2)).then_inc(heads_landed, 16)
                        pool.dma_start(y[0:20, 2, 0:256], dram["c_heads"][:, 1024:1280]).then_inc(heads_landed, 16)
                meet()
                meet()
                rope(range(T_SQ, T_SK + 2))
                meet()
                meet()

            def out1(l):
                pool.dma_start(ple[:, :, :], dram["ple"][l].rearrange("p (a b) -> p a b", a=2)).then_inc(ple_landed, 16)
                add_squares()

            def mix2(l):
                meet()
                if l == 0:
                    pool.dma_start(dil[:, :], dram["c_dilated"]).then_inc(dil_landed, 16)
                rope(range(16))
                if l == 0:
                    pool.wait_ge(dil_landed, c.count(dil_landed, 16))
                meet()
                meet()
                if l == 1:
                    meet()

            def out2(l):
                pool.dma_start(mem[:, :, :], dram["mem"].rearrange("p (a b) -> p a b", a=DT)).then_inc(mem_landed, 16)
                add_squares()

                add_squares(before=lambda k: ahead(k, y_scaled, 0))

            def cross(l):
                meet()
                meet()
                meet()

            def xo(l):
                add_squares()
                add_squares()
                if DT * (6 + 3 * l + 2) > 0:
                    pool.wait_ge(x_ready, DT * (6 + 3 * l + 2))
                pool.memset(y[:, 0:8, :], 0.0)
                pool.drain().then_inc(y_zero, 1)

            def ffn2(l):
                add_squares()
                if l + 1 < LAYERS:
                    add_squares()

            load(0)
            for l in range(LAYERS):
                mix1(l)
                out1(l)
                add_squares()
                add_squares()
                add_squares(before=lambda k: ahead(k, e_gated, 8))
            pool.wait_ge(x_ready, DT * 3 * LAYERS)
            positions("positions_2")
            for l in range(LAYERS):
                mix2(l)
                out2(l)
                cross(l)
                xo(l)
                ffn2(l)


def tiles(a):
    f, s = a.shape
    return a.reshape(f // P, P, s).transpose(1, 0, 2).reshape(P, -1)


def units(w, kt=KU):
    k, n = w.shape
    u = w.reshape(k // P, P, n // P, P).transpose(2, 1, 0, 3).reshape(n // P, P, k)
    if k < KU * P:
        u = np.concatenate([u, np.zeros((n // P, P, KU * P - k), w.dtype)], axis=2)
    return u


def pack_weights(i):
    out = []
    cols = np.array(win_columns())
    for l in range(LAYERS):
        w = np.where(cols[None, :] >= 0, i["w_in"][l][:, np.maximum(cols, 0)], np.float32(0))
        out += [units(w), units(i["w_out"][l])]
        for ch in range(FFN1_CHUNKS):
            part = slice(ch * 1024, ch * 1024 + 1024)
            out += [units(i["w_up"][l][:, part]), units(i["w_down"][l][part])]
        out += [units(i["w_ple_proj"][l]), units(i["w_ple_gate"][l])]
    for l in range(LAYERS):
        mixer = "ab"[l]
        out += [units(i[mixer + "_w_in_2"][0]), units(i[mixer + "_w_out_2"][0]), units(i["x_wkv_2"][l]),
                units(i["x_wq_2"][l]), units(i["x_wo_2"][l])]
        at = 0
        for n in FFN2_CHUNKS:
            part = slice(at * P, (at + n) * P)
            g, u = units(i["w_gate_up_2"][l][:, part]), units(i["w_gate_up_2"][l][:, FF2:][:, part])
            out += [np.stack([g, u], 1).reshape(-1, P, KU * P), units(i["w_down_2"][l][part])]
            at += n
    return np.concatenate(out)


def pack_vectors(i):
    cols = np.array(win_columns())
    vec = np.zeros((P, NV), np.float32)

    def put(name, layer, a):
        base, width = VCOL[name]
        vec[:, base + layer * width:base + (layer + 1) * width] = a

    for l in range(LAYERS):
        put("b_in", l, np.where(cols >= 0, i["b_in"][l][np.maximum(cols, 0)], np.float32(0)).reshape(-1, P).T)
        for name, src in (("in_g", "in_norm_g"), ("mlp_g", "mlp_norm_g"), ("ple_g", "ple_norm_g"), ("post_g", "ple_post_norm_g"),
                          ("conv_b", "mlstm_conv_b"), ("m_g", "mlstm_norm_g"), ("h_g", "hgrn_norm_g"),
                          ("lb_logit", "hgrn_lb_logits"), ("mix_pre", "mix_pre_g_2"), ("mix_post", "mix_post_g_2"),
                          ("mem_pre", "mem_pre_g_2"), ("mem_kv", "mem_kv_g_2"), ("mem_post", "mem_post_g_2"),
                          ("ffn_pre", "ffn_pre_g_2"), ("ffn_post", "ffn_post_g_2")):
            put(name, l, i[src][l].reshape(-1, P).T)
        put("conv_w", l, i["mlstm_conv_w"][l].reshape(16, P).T)
        put("q_g", l, np.tile(i["swa_q_norm_g"][l], 2)[:, None])
        put("k_g", l, np.tile(i["swa_k_norm_g"][l], 2)[:, None])
        put("sinks", l, np.tile(i["swa_sinks"][l], (P, 1)))
        vec[32:36, VCOL["f_b"][0] + l] = i["mlstm_f_bias"][l]
    put("sub_g", 0, i["b_sub_g_2"][0][:, None])
    base = VCOL["lam"][0]
    for j, name in enumerate(("q1", "q2", "k1", "k2")):
        vec[:64, base + j] = i[f"b_lam_{name}_2"][0]
    freq = np.zeros(64, np.float32)
    freq[0:8] = freq[8:16] = (500000.0 ** (-np.arange(0, 16, 2) / 16.0)).astype(np.float32)
    vec[:, VCOL["inv_freq"][0]] = np.tile(freq, 2)
    return vec


def kernel(**inputs):
    import concourse.bacc as bacc
    from concourse.bass_utils import run_bass_kernel_spmd as run

    i = {k: np.asarray(a) for k, a in inputs.items()}
    arrays = dict(constants(), weights=pack_weights(i), vec=pack_vectors(i), x=tiles(i["x"][0].T), mem=tiles(i["mem_2"][0].T),
                  ple=np.stack([tiles(i["p"][l, 0].T) for l in range(LAYERS)]),
                  positions=i["positions"][0], positions_2=i["positions_2"][0])
    arrays = {k: np.ascontiguousarray(a) for k, a in arrays.items()}
    nc = bacc.Bacc("TRN2", target_bir_lowering=False, num_devices=1)
    dram = {k: nc.dram_tensor(k, a.shape, mybir.dt.from_np(a.dtype), kind="ExternalInput").ap() for k, a in arrays.items()}
    out = nc.dram_tensor("out", (P, DT * S), F32, kind="ExternalOutput").ap()
    build(nc, dram, out)
    r = run(nc, [arrays], core_ids=[0])
    got = r.results[0]["out"]
    return got.reshape(P, DT, S).transpose(2, 1, 0).reshape(1, S, D)
```
